# Optimizing a Trainium2 kernel written in Bass

```python
import math
import jax, jax.numpy as jnp
from jax import lax
import numpy as np

D_MODEL = 1024
BATCH = 1
SEQ = 512
DEPTH = 1

N_META = 16
BLOCK = 128
META_PAD = BLOCK - N_META
RET_HEADS = 4
RET_DK = D_MODEL // 8
RET_DV = D_MODEL // 4
DIFF_HEADS = 8
DIFF_HD = D_MODEL // 16
DIFF_VD = 2 * DIFF_HD
CONV_WIDTH = D_MODEL
CONV_K = 3
N_BRANCH = 3
BRANCH_W = D_MODEL
D_FF = 4 * D_MODEL
EPS = 1e-6
NEG_INF = -1e30
IN_WIDTHS = (RET_HEADS * RET_DK, RET_HEADS * RET_DK, RET_HEADS * RET_DV, RET_HEADS * RET_DV,
             2 * DIFF_HEADS * DIFF_HD, 2 * DIFF_HEADS * DIFF_HD, DIFF_HEADS * DIFF_VD,
             CONV_WIDTH, CONV_WIDTH, CONV_WIDTH, N_BRANCH * D_MODEL)
D_IN = sum(IN_WIDTHS)


def rms_norm(x, w):
    xf = x.astype(jnp.float32)
    y = xf * lax.rsqrt(jnp.mean(xf * xf, axis=-1, keepdims=True) + EPS)
    return (y * w.astype(jnp.float32)).astype(x.dtype)

def head_layer_norm(y):
    yf = y.astype(jnp.float32)
    mu = jnp.mean(yf, axis=-1, keepdims=True)
    var = jnp.mean(jnp.square(yf - mu), axis=-1, keepdims=True)
    return ((yf - mu) * lax.rsqrt(var + EPS)).astype(y.dtype)

def pad_front(t, n):
    return jnp.pad(t, [(0, 0), (n, 0)] + [(0, 0)] * (t.ndim - 2))

def column_bounds():
    bounds, start = [], 0
    for w in IN_WIDTHS:
        bounds.append((start, start + w))
        start += w
    return bounds

def retention(q, k, v):
    b = q.shape[0]
    dt = q.dtype
    k = k * (RET_DK ** -0.5)
    q, k, v = (pad_front(t, META_PAD) for t in (q, k, v))
    nc = q.shape[1] // BLOCK

    def chunks(t):
        return t.reshape(b, nc, BLOCK, RET_HEADS, t.shape[-1]).transpose(1, 0, 3, 2, 4)

    log_g = jnp.log1p(-jnp.exp2(-5.0 - jnp.arange(RET_HEADS, dtype=jnp.float32)))
    i = jnp.arange(BLOCK, dtype=jnp.float32)
    dist = i[:, None] - i[None, :]
    intra = jnp.where(dist >= 0, jnp.exp(log_g[:, None, None] * jnp.maximum(dist, 0.0)), 0.0).astype(dt)
    q_decay = jnp.exp(log_g[:, None] * (i + 1.0)).astype(dt)
    k_decay = jnp.exp(log_g[:, None] * (BLOCK - 1.0 - i)).astype(dt)
    s_decay = jnp.exp(log_g * BLOCK).astype(dt)

    def step(state, qkv):
        qc, kc, vc = qkv
        scores = jnp.einsum('bhid,bhjd->bhij', qc, kc) * intra
        out = (jnp.einsum('bhij,bhjv->bhiv', scores, vc)
               + jnp.einsum('bhid,bhdv->bhiv', qc * q_decay[:, :, None], state))
        state = state * s_decay[:, None, None] + jnp.einsum('bhjd,bhjv->bhdv', kc * k_decay[:, :, None], vc)
        return state, out

    s0 = jnp.zeros((b, RET_HEADS, RET_DK, RET_DV), dt)
    _, out = lax.scan(step, s0, (chunks(q), chunks(k), chunks(v)))
    out = out.transpose(1, 0, 3, 2, 4).reshape(b, nc * BLOCK, RET_HEADS, RET_DV)
    return out[:, META_PAD:]

def diff_attention(q, k, v, lam, subln_w, lam_init):
    b = q.shape[0]
    q, k, v = (pad_front(t, META_PAD) for t in (q, k, v))
    p = q.shape[1]
    nb = p // BLOCK
    kt = k.transpose(0, 2, 3, 1, 4)
    vt = v.transpose(0, 2, 1, 3)
    qb = q.reshape(b, nb, BLOCK, DIFF_HEADS, 2, DIFF_HD).transpose(1, 0, 3, 4, 2, 5)
    slopes = jnp.exp2(-8.0 / DIFF_HEADS * (jnp.arange(DIFF_HEADS, dtype=jnp.float32) + 1.0))
    kpos = jnp.arange(p)
    scale = DIFF_HD ** -0.5

    def block(args):
        qblk, bi = args
        qpos = bi * BLOCK + jnp.arange(BLOCK)
        dist = (qpos[:, None] - kpos[None, :]).astype(jnp.float32)
        valid = (dist >= 0) & (kpos[None, :] >= META_PAD)
        logits = (jnp.einsum('bhmqd,bhmkd->bhmqk', qblk, kt, preferred_element_type=jnp.float32) * scale
                  - slopes[:, None, None, None] * dist)
        probs = jax.nn.softmax(jnp.where(valid, logits, NEG_INF), axis=-1)
        attn = probs[:, :, 0] - lam * probs[:, :, 1]
        return jnp.einsum('bhqk,bhkv->bhqv', attn.astype(vt.dtype), vt)

    out = lax.map(block, (qb, jnp.arange(nb)))
    out = out.transpose(1, 0, 3, 2, 4).reshape(b, p, DIFF_HEADS, DIFF_VD)[:, META_PAD:]
    return rms_norm(out, subln_w) * (1.0 - lam_init)

def short_conv(u, w):
    return lax.conv_general_dilated(
        u, w[:, None, :].astype(u.dtype), window_strides=(1,), padding=[(CONV_K - 1, 0)],
        dimension_numbers=('NWC', 'WIO', 'NWC'), feature_group_count=u.shape[-1])

def hybrid_layer(x, layer, norm1_w, w_in, conv_w, lam_vecs, subln_w, w_branch, w_out, norm2_w, w_up, w_down):
    b, l, _ = x.shape
    h = rms_norm(x, norm1_w)
    (rq, rk, rv, rg, dq, dk, dv, cb, cc, cx, gates) = [h @ w_in[:, s:e] for s, e in column_bounds()]

    ret = retention(rq.reshape(b, l, RET_HEADS, RET_DK), rk.reshape(b, l, RET_HEADS, RET_DK),
                    rv.reshape(b, l, RET_HEADS, RET_DV))
    ret = head_layer_norm(ret).reshape(b, l, BRANCH_W) * jax.nn.silu(rg)

    lam_init = 0.8 - 0.6 * math.exp(-0.3 * layer)
    lv = lam_vecs.astype(jnp.float32)
    lam = jnp.exp(jnp.sum(lv[0] * lv[1])) - jnp.exp(jnp.sum(lv[2] * lv[3])) + lam_init
    diff = diff_attention(dq.reshape(b, l, DIFF_HEADS, 2, DIFF_HD), dk.reshape(b, l, DIFF_HEADS, 2, DIFF_HD),
                          dv.reshape(b, l, DIFF_HEADS, DIFF_VD), lam, subln_w, lam_init).reshape(b, l, BRANCH_W)

    conv = cb * short_conv(cc * cx, conv_w)

    g = jax.nn.sigmoid(gates.astype(jnp.float32)).astype(x.dtype).reshape(b, l, N_BRANCH, D_MODEL)
    merged = (g[:, :, 0] * (ret @ w_branch[0]) + g[:, :, 1] * (diff @ w_branch[1])
              + g[:, :, 2] * (conv @ w_branch[2]))
    x = x + merged @ w_out

    u = jnp.square(jax.nn.relu(rms_norm(x, norm2_w) @ w_up))
    return x + u @ w_down

def first_inputs(seed: int = 0) -> dict:
    key = jax.random.key(seed)
    ks = jax.random.split(key, 13)
    nrm = jax.random.normal
    f32 = jnp.float32
    return {
        "x": nrm(ks[0], (BATCH, SEQ, D_MODEL), f32),
        "meta_tokens": nrm(ks[1], (N_META, D_MODEL), f32),
        "norm1_w": 1.0 + 0.02 * nrm(ks[2], (DEPTH, D_MODEL), f32),
        "w_in": nrm(ks[3], (DEPTH, D_MODEL, D_IN), f32) * D_MODEL ** -0.5,
        "conv_w": nrm(ks[4], (DEPTH, CONV_K, CONV_WIDTH), f32) * CONV_K ** -0.5,
        "diff_lambda": 0.1 * nrm(ks[5], (DEPTH, 4, DIFF_HD), f32),
        "diff_subln_w": 1.0 + 0.02 * nrm(ks[6], (DEPTH, DIFF_VD), f32),
        "w_branch": nrm(ks[7], (DEPTH, N_BRANCH, BRANCH_W, D_MODEL), f32) * BRANCH_W ** -0.5,
        "w_out": nrm(ks[8], (DEPTH, D_MODEL, D_MODEL), f32) * D_MODEL ** -0.5,
        "norm2_w": 1.0 + 0.02 * nrm(ks[9], (DEPTH, D_MODEL), f32),
        "w_up": nrm(ks[10], (DEPTH, D_MODEL, D_FF), f32) * D_MODEL ** -0.5,
        "w_down": nrm(ks[11], (DEPTH, D_FF, D_MODEL), f32) * D_FF ** -0.5,
        "final_norm_w": 1.0 + 0.02 * nrm(ks[12], (D_MODEL,), f32),
    }

def first_block(x, meta_tokens, norm1_w, w_in, conv_w, diff_lambda, diff_subln_w, w_branch, w_out,
              norm2_w, w_up, w_down, final_norm_w):
    b = x.shape[0]
    meta = jnp.broadcast_to(meta_tokens.astype(x.dtype)[None], (b, N_META, D_MODEL))
    h = jnp.concatenate([meta, x], axis=1)
    for layer in range(DEPTH):
        h = hybrid_layer(h, layer, norm1_w[layer], w_in[layer], conv_w[layer], diff_lambda[layer],
                         diff_subln_w[layer], w_branch[layer], w_out[layer], norm2_w[layer],
                         w_up[layer], w_down[layer])
    return rms_norm(h[:, N_META:], final_norm_w)


CHUNK = 64
Q_BLOCK = 128
SB_HEADS = 8
SB_HEAD_DIM = 64
GLA_HEADS = 4
GLA_HEAD_DK = 128
GLA_HEAD_DV = 256
GATE_RANK = 16
GATE_TAU = 16.0
D_FF_2 = 2816
CONV_W = 3
N_BRANCHES = 2

SB_WIDTH = SB_HEADS * SB_HEAD_DIM
GLA_K_WIDTH = GLA_HEADS * GLA_HEAD_DK
GLA_V_WIDTH = GLA_HEADS * GLA_HEAD_DV
IN_WIDTHS_2 = (SB_WIDTH, SB_WIDTH, SB_WIDTH, GLA_K_WIDTH, GLA_K_WIDTH, GLA_V_WIDTH, GLA_V_WIDTH, GATE_RANK, N_BRANCHES * D_MODEL)
IN_TOTAL = 3 * SB_WIDTH + 2 * GLA_K_WIDTH + 2 * GLA_V_WIDTH + GATE_RANK + N_BRANCHES * D_MODEL


def _rmsnorm(x, g):
    xf = x.astype(jnp.float32)
    y = xf * lax.rsqrt(jnp.mean(xf * xf, axis=-1, keepdims=True) + EPS)
    return (y * g.astype(jnp.float32)).astype(x.dtype)

def _split_cols(a, widths):
    outs, start = [], 0
    for w in widths:
        outs.append(a[..., start:start + w])
        start += w
    return outs

def _heads(a, n_heads):
    b, l, _ = a.shape
    return a.reshape(b, l, n_heads, -1).transpose(0, 2, 1, 3)

def _stick_breaking(q, k, v):
    b, h, lp, dh = q.shape
    nb = lp // Q_BLOCK
    scale = dh ** -0.5
    kpos = jnp.arange(lp)
    qb = q.reshape(b, h, nb, Q_BLOCK, dh).transpose(2, 0, 1, 3, 4)

    def block(args):
        qi, i = args
        z = jnp.einsum('bhqd,bhkd->bhqk', qi, k).astype(jnp.float32) * scale
        qpos = i * Q_BLOCK + jnp.arange(Q_BLOCK)
        strict = kpos[None, :] < qpos[:, None]
        u = jnp.where(strict, jax.nn.log_sigmoid(-z), 0.0)
        tail = lax.cumsum(u, axis=3, reverse=True) - u
        w = jnp.where(strict, jnp.exp(jax.nn.log_sigmoid(z) + tail), 0.0)
        return jnp.einsum('bhqk,bhkd->bhqd', w.astype(v.dtype), v)

    out = lax.map(block, (qb, jnp.arange(nb)))
    return out.transpose(1, 2, 0, 3, 4).reshape(b, h, lp, dh)

def _gla(q, k, v, g):
    b, h, lp, dk = q.shape
    dv = v.shape[-1]
    nc = lp // CHUNK

    def to_chunks(a):
        return a.reshape(b, h, nc, CHUNK, a.shape[-1]).transpose(2, 0, 1, 3, 4)

    qc, kc, vc, gc = to_chunks(q), to_chunks(k), to_chunks(v), to_chunks(g)
    causal = jnp.tril(jnp.ones((CHUNK, CHUNK), dtype=bool))

    def step(state, inp):
        qi, ki, vi, gi = inp
        cum = jnp.cumsum(gi, axis=2)
        diff = cum[:, :, :, None, :] - cum[:, :, None, :, :]
        decay = jnp.exp(jnp.where(causal[None, None, :, :, None], diff, -jnp.inf))
        att = jnp.einsum('bhtd,bhsd,bhtsd->bhts', qi, ki, decay)
        o = jnp.einsum('bhts,bhsv->bhtv', att, vi) + jnp.einsum('bhtd,bhdv->bhtv', qi * jnp.exp(cum), state)
        last = cum[:, :, -1:, :]
        state = jnp.exp(last[:, :, 0, :])[..., None] * state + jnp.einsum('bhsd,bhsv->bhdv', ki * jnp.exp(last - cum), vi)
        return state, o

    state0 = jnp.zeros((b, h, dk, dv), jnp.float32)
    _, oc = lax.scan(step, state0, (qc, kc, vc, gc))
    return oc.transpose(1, 2, 0, 3, 4).reshape(b, h, lp, dv)

def _causal_dwconv(a, w, bias):
    a_p = jnp.pad(a, ((0, 0), (CONV_W - 1, 0), (0, 0)))
    y = lax.conv_general_dilated(a_p, w[:, None, :].astype(a.dtype), window_strides=(1,), padding='VALID',
                                 dimension_numbers=('NWC', 'WIO', 'NWC'), feature_group_count=a.shape[-1])
    return y + bias.astype(a.dtype)

def second_inputs(seed: int = 0) -> dict:
    key = jax.random.key(seed)
    ks = jax.random.split(key, 20)
    f32 = jnp.float32

    def nrm(k, shape, scale):
        return jax.random.normal(k, shape, f32) * scale

    def gain(k, n):
        return 1.0 + 0.02 * jax.random.normal(k, (DEPTH, n), f32)

    return {
        "x": nrm(ks[0], (BATCH, SEQ, D_MODEL), 1.0),
        "meta_tokens": nrm(ks[1], (N_META, D_MODEL), 1.0),
        "norm_mix_pre": gain(ks[2], D_MODEL),
        "w_in": nrm(ks[3], (DEPTH, D_MODEL, IN_TOTAL), D_MODEL ** -0.5),
        "w_gk_up": nrm(ks[4], (DEPTH, GATE_RANK, GLA_K_WIDTH), GATE_RANK ** -0.5),
        "b_gk": nrm(ks[5], (DEPTH, GLA_K_WIDTH), 0.1),
        "gla_head_norm": gain(ks[6], GLA_HEAD_DV),
        "w_sb_out": nrm(ks[7], (DEPTH, SB_WIDTH, D_MODEL), SB_WIDTH ** -0.5),
        "w_gla_out": nrm(ks[8], (DEPTH, GLA_V_WIDTH, D_MODEL), GLA_V_WIDTH ** -0.5),
        "w_o": nrm(ks[9], (DEPTH, D_MODEL, D_MODEL), D_MODEL ** -0.5),
        "norm_mix_post": gain(ks[10], D_MODEL),
        "norm_ffn_pre": gain(ks[11], D_MODEL),
        "w_ffn_up": nrm(ks[12], (DEPTH, D_MODEL, D_FF_2), D_MODEL ** -0.5),
        "w_ffn_gate": nrm(ks[13], (DEPTH, D_MODEL, D_FF_2), D_MODEL ** -0.5),
        "conv_w": nrm(ks[14], (DEPTH, CONV_W, D_FF_2), CONV_W ** -0.5),
        "conv_b": nrm(ks[15], (DEPTH, D_FF_2), 0.02),
        "w_ffn_down": nrm(ks[16], (DEPTH, D_FF_2, D_MODEL), D_FF_2 ** -0.5),
        "norm_ffn_post": gain(ks[17], D_MODEL),
    }

def second_block(x, meta_tokens, norm_mix_pre, w_in, w_gk_up, b_gk, gla_head_norm, w_sb_out, w_gla_out, w_o,
              norm_mix_post, norm_ffn_pre, w_ffn_up, w_ffn_gate, conv_w, conv_b, w_ffn_down, norm_ffn_post):
    b, s, _ = x.shape
    L = s + N_META
    Lp = -(-L // Q_BLOCK) * Q_BLOCK
    meta = jnp.broadcast_to(meta_tokens[None].astype(x.dtype), (b, N_META, D_MODEL))
    h = jnp.concatenate([meta, x], axis=1)

    for l in range(DEPTH):
        hn = _rmsnorm(h, norm_mix_pre[l])
        hn_p = jnp.pad(hn, ((0, 0), (0, Lp - L), (0, 0)))
        proj = hn_p @ w_in[l]
        sb_q, sb_k, sb_v, g_q, g_k, g_v, g_r, g_lr, merge = _split_cols(proj, IN_WIDTHS_2)

        sb = _stick_breaking(_heads(sb_q, SB_HEADS), _heads(sb_k, SB_HEADS), _heads(sb_v, SB_HEADS))
        sb = sb.transpose(0, 2, 1, 3).reshape(b, Lp, SB_WIDTH)[:, :L]

        glog = jax.nn.log_sigmoid((g_lr @ w_gk_up[l] + b_gk[l]).astype(jnp.float32)) / GATE_TAU
        gq = _heads(g_q, GLA_HEADS).astype(jnp.float32) * (GLA_HEAD_DK ** -0.5)
        gk = _heads(g_k, GLA_HEADS).astype(jnp.float32)
        gv = _heads(g_v, GLA_HEADS).astype(jnp.float32)
        o = _gla(gq, gk, gv, _heads(glog, GLA_HEADS))
        o = _rmsnorm(o, gla_head_norm[l])
        o = o.transpose(0, 2, 1, 3).reshape(b, Lp, GLA_V_WIDTH)[:, :L].astype(h.dtype)
        o = o * jax.nn.silu(g_r[:, :L])

        gates = jax.nn.sigmoid(merge[:, :L])
        gate_sb, gate_gla = gates[..., :D_MODEL], gates[..., D_MODEL:]
        mix = (gate_sb * (sb @ w_sb_out[l]) + gate_gla * (o @ w_gla_out[l])) @ w_o[l]
        h = h + _rmsnorm(mix, norm_mix_post[l])

        hn = _rmsnorm(h, norm_ffn_pre[l])
        up = hn @ w_ffn_up[l]
        act = jax.nn.gelu(_causal_dwconv(up, conv_w[l], conv_b[l]), approximate=True)
        ffn = (act * (hn @ w_ffn_gate[l])) @ w_ffn_down[l]
        h = h + _rmsnorm(ffn, norm_ffn_post[l])

    return h[:, N_META:]


def setup_inputs(seed=0):
    out = dict(first_inputs(seed))
    for name, value in second_inputs(seed + 1).items():
        if name != "x":
            out[name + "_2"] = value
    return out


def reference(
    x, meta_tokens, norm1_w, w_in, conv_w, diff_lambda, diff_subln_w, w_branch, w_out, norm2_w,
    w_up, w_down, final_norm_w, meta_tokens_2, norm_mix_pre_2, w_in_2, w_gk_up_2, b_gk_2,
    gla_head_norm_2, w_sb_out_2, w_gla_out_2, w_o_2, norm_mix_post_2, norm_ffn_pre_2,
    w_ffn_up_2, w_ffn_gate_2, conv_w_2, conv_b_2, w_ffn_down_2, norm_ffn_post_2,
):
    x = first_block(
        x, meta_tokens, norm1_w, w_in, conv_w, diff_lambda, diff_subln_w, w_branch, w_out,
        norm2_w, w_up, w_down, final_norm_w,
    )
    return second_block(
        x, meta_tokens_2, norm_mix_pre_2, w_in_2, w_gk_up_2, b_gk_2, gla_head_norm_2,
        w_sb_out_2, w_gla_out_2, w_o_2, norm_mix_post_2, norm_ffn_pre_2, w_ffn_up_2,
        w_ffn_gate_2, conv_w_2, conv_b_2, w_ffn_down_2, norm_ffn_post_2,
    )


_drawn_inputs = setup_inputs


def setup_inputs(seed=0):
    import zlib

    import numpy as np

    out = dict(_drawn_inputs(seed))
    spreads = {}
    factors = {'diff_subln_w': 4.377,
     'gla_head_norm_2': 5.211,
     'norm_mix_post_2': 3.504,
     'norm_ffn_pre_2': 3.202,
     'conv_b_2': 5.115,
     'norm_ffn_post_2': 4.911}
    for name, (base, spread) in spreads.items():
        noise = np.random.default_rng([zlib.crc32(name.encode()), seed]).standard_normal(out[name].shape)
        drawn = base * np.exp(spread * noise) if base else spread * noise
        out[name] = __import__('jax').numpy.asarray(drawn.astype(out[name].dtype))
    for name, factor in factors.items():
        out[name] = (out[name] * factor).astype(out[name].dtype)
    return out
```

```python
from contextlib import ExitStack, contextmanager

import numpy as np

import concourse.bass as bass
from concourse import mybir

F32 = mybir.dt.float32
F32R = mybir.dt.float32r
BF16 = mybir.dt.bfloat16
ALU = mybir.AluOpType
ACT = mybir.ActivationFunctionType
AX = mybir.AxisListType.X

P = 128
D = 1024
KC = D // P
NM = 16
SEQ = 512
T = NM + SEQ
HALF = T // 2
EPS = 1e-6
RH, RDV = 4, 256
DH, DHD = 8, 64
LAM_INIT = 0.2
FF1 = 4 * D
SH, SHD = 8, 64
GH, GDV = 4, 256
GATE_TAU = 16.0
FF2 = 2816
FT2 = FF2 // P

COLS = {}
for _name, _n in (("norm1_w", 8), ("norm2_w", 8), ("final_norm_w", 8), ("diff_subln_w", 1), ("conv_w", 24),
                  ("norm_mix_pre_2", 8), ("gla_head_norm_2", 2), ("norm_mix_post_2", 8), ("norm_ffn_pre_2", 8),
                  ("norm_ffn_post_2", 8), ("conv_w_2", 3 * FT2), ("conv_b_2", FT2), ("b_gk_2", 4)):
    COLS[_name] = (sum(n for _, n in COLS.values()), _n)
NCOL = sum(n for _, n in COLS.values())

FFN2_GROUPS = (8, 8, 6)
PHASES = [("conv_in", 24), ("conv_out", 16), ("ret_qkv", 16), ("ret_gate", 8), ("ret_out", 16), ("diff_qkv", 24),
          ("diff_out", 16), ("w_out", 8)]
PHASES += [(f"ffn{g}{s}", 8) for g in range(4) for s in ("up", "down")]
PHASES += [("sb_qkv", 12), ("sb_out", 16), ("gla_lr", 1), ("gla_qkv", 16), ("gla_gate", 8), ("gla_out", 16),
           ("w_o", 8)]
for _g, _n in enumerate(FFN2_GROUPS):
    PHASES += [(f"glu{_g}up", 2 * _n), (f"glu{_g}down", 8)]
START = {}
for _name, _n in PHASES:
    START[_name] = sum(p[1] for p in PHASES[:len(START)])
NSTRIP = sum(p[1] for p in PHASES)


def pos(base, k=0, i=0, step=2):
    return base + k + step * i, (base + k) // 2 + (step // 2) * i, (base + k) % 2


def flat(ap):
    return ap.rearrange("p a t -> p (a t)")


class Link:

    def __init__(self, eng, sem):
        self.eng, self.sem, self.base, self.n = eng, sem, 0, 0

    def __call__(self, ins):
        ins.then_inc(self.sem, 1)
        self.n += 1
        self.eng.wait_ge(self.sem, self.base + self.n)

    @contextmanager
    def loop(self, count, per):
        before = self.base + self.n
        with self.eng.Fori(0, count) as i:
            self.base, self.n = before + i * per, 0
            yield i
            assert self.n == per, (self.n, per)
        self.base, self.n = before + count * per, 0


def two(ap):
    return ap.rearrange("p (h t) -> p h t", h=2)


def build(nc, weights, cols, tables, consts, lam_rows, x_t, meta2_t, wgk, gla_masks, res_dram, out):
    ctx = ExitStack()
    with ctx:
        def sb(name, shape, dt=F32):
            return ctx.enter_context(nc.sbuf_tensor(name, shape, dt))

        def sem(name):
            return ctx.enter_context(nc.semaphore(name))

        xh, xl = sb("xh", [P, KC, T], F32R), sb("xl", [P, KC, T], F32R)
        bh, bl = sb("bh", [P, KC, T], F32R), sb("bl", [P, KC, T], F32R)
        wraw = sb("wraw", [P, 2, KC, P])
        wh, wl = sb("wh", [P, 2, KC, P], F32R), sb("wl", [P, 2, KC, P], F32R)
        qq, kk = sb("qq", [P, KC, T]), sb("kk", [P, KC, T])
        vt = sb("vt", [P, 5, D])
        mrg = sb("mrg", [P, KC, T])
        res = sb("res", [P, KC, T])
        tmp = sb("tmp", [P, 2, T])
        hf = sb("hf", [P, 2, T])
        gate = sb("gate", [P, T])
        rsq = gate
        cst = sb("cst", [P, 4, P])
        ident, ones, ntri, nones = (cst[:, i, :] for i in range(4))
        col = sb("col", [P, NCOL])
        small = sb("small", [P, 8])
        stat = sb("stat", [P, 16])
        xrows = sb("xrows", [P, 5, T])
        glm = sb("glm", [P, 8, P])
        negm = sb("negm", [P, P], BF16)
        identb = sb("identb", [P, P], BF16)
        lrw = sb("lrw", [NM, 4 * P])
        lamr = sb("lamr", [P, 4 * DHD])
        ps = ctx.enter_context(nc.psum_tensor("ps", [P, 8, 512], F32))

        scr = res[:, :, :].rearrange("p c t -> p (c t)")
        SBW = 4 * P + 3 * P + 2 * P + P
        sbt = [scr[:, (SBW + T) * k:(SBW + T) * k + SBW] for k in range(2)]
        sbm = [scr[0:NM, (SBW + T) * k + SBW:(SBW + T) * (k + 1)] for k in range(2)]
        SB0 = (0, 512, 896, 1152)
        srow = [res[:, k, :] for k in range(8)]
        xl_rows = [xrows[:, k, :] for k in range(5)] + srow[0:2]
        cum, qc, kh, grow, gtmp = srow[2], srow[3], srow[4], (srow[5], srow[6]), srow[7]
        masked = hf[:, :, :].rearrange("p a t -> p (a t)")[:, 0:8 * P].rearrange("p (l t) -> p l t", l=8)
        amat = [tmp[:, 0, P * k:P * k + P] for k in range(2)]
        ktok = [tmp[:, 1, P * k:P * k + P] for k in range(2)]
        state = [gate[:, GDV * k:GDV * k + GDV] for k in range(2)]
        at = scr[:, 0:2048].rearrange("p (k q) -> p k q", k=4)
        atm = scr[:, 2048:2560]
        prob = [[scr[:, 2560 + T * m:2560 + T * (m + 1)] for m in range(2)],
                [scr[:, 2560 + 2 * T:2560 + 3 * T], gate[:, :]]]
        tbl = [hf[:, 0, :], hf[:, 1, :]]

        def wcol(name, i=0):
            o = COLS[name][0] + i
            return col[:, o:o + 1] if isinstance(i, int) else col[:, bass.ds(o, 1)]

        w_loaded = [sem("w_loaded0"), sem("w_loaded1")]
        hi_done, lo_done = sem("hi_done"), sem("lo_done")
        mm_done = sem("mm_done")
        evicted = [sem("evicted0"), sem("evicted1")]
        x_ready, b_ready = sem("x_ready"), sem("b_ready")
        act_self, dve_self = sem("act_self"), sem("dve_self")
        params_in, x_in, table_in, res_in = sem("params_in"), sem("x_in"), sem("table_in"), sem("res_in")
        table_in = [sem("table_in0"), sem("table_in1")]
        sq_ready, sq_used = sem("sq_ready"), sem("sq_used")
        root_ready = sem("root_ready")
        rs_ready = sem("rs_ready")
        hf_ready, hf_hi = sem("hf_ready"), sem("hf_hi")
        relu_ready = sem("relu_ready")
        vtr_done, vt_done = sem("vtr_done"), sem("vt_done")
        lam_sums, lam_exps, eps_set = sem("lam_sums"), sem("lam_exps"), sem("eps_set")
        rz_ready, rs_masked, ro_ready, ro_copied = (sem(n) for n in ("rz_ready", "rs_masked", "ro_ready", "ro_copied"))
        mean_ready, centred = sem("mean_ready"), sem("centred")
        dz_ready, ds_ready, dmax_ready, dp_ready, da_ready, dt_ready, dt_copied, do_ready, do_copied = (
            sem(n) for n in ("dz_ready", "ds_ready", "dmax_ready", "dp_ready", "da_ready", "dt_ready", "dt_copied",
                             "do_ready", "do_copied"))
        mrg_ready, mrg_sum = sem("mrg_ready"), sem("mrg_sum")
        stored = sem("stored")
        h_ready, meta_in, res_saved, res_back = (sem(n) for n in ("h_ready", "meta_in", "res_saved", "res_back"))
        const2_in, masks_made, pool_self = sem("const2_in"), sem("masks_made"), sem("pool_self")
        sz_ready, sabs_done, slog_done, sp_done, scum_done, sw_done, so_ready, so_hi = (sem(n) for n in (
            "sz_ready", "sabs_done", "slog_done", "sp_done", "scum_done", "sw_done", "so_ready", "so_hi"))
        lr_ready, gy_ready, gy_abs, gy_log, glog_done = (sem(n) for n in (
            "lr_ready", "gy_ready", "gy_abs", "gy_log", "glog_done"))
        gcum_done, gexp_done, gd_ready, ge_ready, gx_ready = (sem(n) for n in (
            "gcum_done", "gexp_done", "gd_ready", "ge_ready", "gx_ready"))
        gp_ready, gp_used, ga_ready, gt_ready, gt_copied, gs_ready, gs_done, go_ready, go_copied = (sem(n) for n in (
            "gp_ready", "gp_used", "ga_ready", "gt_ready", "gt_copied", "gs_ready", "gs_done", "go_ready",
            "go_copied"))
        mix_added, glu_copied, glu_act, out_ready = (sem(n) for n in ("mix_added", "glu_copied", "glu_act",
                                                                      "out_ready"))

        def slot_ap(slot, n):
            return ps[:, 2 * slot, :] if n == SEQ else ps[:, 2 * slot:2 * slot + 2, 0:HALF]

        def row(ap, n):
            return ap[:, NM:T] if n == SEQ else two(ap)

        def key_tiles():
            return [(0, 0)] + [(kb + 1, P * kb) for kb in range(4)]

        def stick_pieces(h):
            k, z = h % 2, 4 * (h % 2)
            return ((sbm[k][:, NM:T], ps[0:NM, z, :]),
                    (sbm[k][:, 0:NM], ps[0:NM, z + 3, 384:384 + NM]),
                    (sbt[k][:, 0:512], ps[:, z + 1, :]),
                    (sbt[k][:, 512:SBW].rearrange("p (b q) -> p b q", b=2), ps[:, z + 2:z + 4, 0:384]))

        def otile(h, v):
            return (4 + 2 * h + v) % 8

        def levels():
            return [(k, L, 0 if L <= NM // 2 else NM) for k, L in enumerate((64, 32, 16, 8, 4, 2, 1))]

        def halves(r, L, lo):
            return r[:, lo:T].rearrange("p (n s l) -> p n s l", s=2, l=L)

        def chunk(c):
            return (slice(0, NM), NM) if c == 0 else (slice(NM + P * (c - 1), NM + P * c), P)

        n_strips = NSTRIP + 1

        N_ROOTS = 1 + RH + DH + 3
        block = ctx.enter_context(nc.Block())

        @block.sync
        def _(sp):
            def load(n, slot):
                sp.dma_start(wraw[:, slot], weights[bass.ds(n, 1)].rearrange("a p k n -> p (a k) n"))\
                    .then_inc(w_loaded[slot], 16)

            for n in range(2):
                load(n, n)
            with sp.Fori(1, n_strips // 2) as i:
                for k in range(2):
                    sp.wait_ge(lo_done, 2 * i + k - 1)
                    load(2 * i + k, k)
            if n_strips % 2:
                sp.wait_ge(lo_done, n_strips - 2)
                load(n_strips - 1, 0)

        @block.scalar
        def _(act):
            link = Link(act, act_self)
            n_hi = n_sq = n_root = 0

            def split_hi(n, half, slot):
                act.wait_ge(w_loaded[slot], 16 * half + 16)
                if not (isinstance(n, int) and n < 2):
                    act.wait_ge(mm_done, n - 1)
                nc.scalar.activation(wh[:, slot], wraw[:, slot], ACT.Copy).then_inc(hi_done, 1)

            def begin(n_half_slot, next_one):
                split_hi(*next_one)
                act.wait_ge(mm_done, n_half_slot[0] + 1)

            def hi_of(dst, src):
                nc.scalar.activation(dst, src, ACT.Copy).then_inc(hf_hi, 1)

            def sum_squares(src, wait):
                nonlocal n_sq
                wait()
                if n_sq >= 2:
                    act.wait_ge(sq_used, n_sq - 1)
                tok = slice(T - src.shape[-1], T)
                nc.scalar.activation(tmp[:, n_sq % 2, tok], src, ACT.Square).then_inc(sq_ready, 1)
                n_sq += 1

            def root(dst, src, scale):
                nonlocal n_root
                nc.scalar.activation(dst, src, ACT.Sqrt, bias=small[:, 0:1], scale=scale).then_inc(root_ready, 1)
                n_root += 1

            def norm(src, n, wait=lambda c: None):
                for c in range(KC):
                    sum_squares(src[:, c, T - n:T], lambda: wait(c))
                act.wait_ge(sq_used, n_sq)
                root(row(rsq, n), ps[:, 4, :] if n == SEQ else ps[:, 4:6, 0:HALF], 1.0 / D)

            def norm_hi(n):
                nonlocal n_hi
                for c in range(KC):
                    act.wait_ge(hf_ready, n_hf + c + 1)
                    hi_of(xh[:, c, T - n:T], hf[:, c % 2, T - n:T])
                n_hi += KC

            act.dma_start(cst[:], consts).then_inc(params_in, 16)
            act.dma_start(col[:], cols).then_inc(params_in, 16)
            act.dma_start(lamr[:], lam_rows).then_inc(params_in, 16)
            for g in range(2):
                act.dma_start(res[:, 4 * g:4 * g + 4], x_t[:, 4 * g:4 * g + 4]).then_inc(x_in, 16)
            act.wait_ge(lam_sums, 2)
            nc.scalar.activation(small[:, 3:5], small[:, 1:3], ACT.Exp).then_inc(lam_exps, 1)
            act.wait_ge(x_in, 32)
            act.wait_ge(eps_set, 1)
            n_hf = 0

            norm(res, T)
            split_hi(0, 0, 0)
            norm_hi(T)
            n_hf += KC

            B = START["conv_in"]
            with act.Fori(0, KC // 2) as i:
                for j in range(2):
                    n, half, slot = pos(B, 3 * j, i, 6)
                    begin((n,), pos(B, 3 * j + 1, i, 6))
                    _, half1, slot1 = pos(B, 3 * j - 2, i, 6)
                    act.wait_ge(evicted[slot1], half1 + 1)
                    nc.scalar.activation(two(gate[:, :]), slot_ap(slot, T), ACT.Copy).then_inc(evicted[slot], 1)
                    split_hi(*pos(B, 3 * j + 2, i, 6))
                    split_hi(*pos(B, 3 * j + 3, i, 6))
                    n2, half2, slot2 = pos(B, 3 * j + 2, i, 6)
                    act.wait_ge(evicted[slot2], half2 + 1)
                    hi_of(flat(bh[:, bass.ds(2 * i + j, 1), NM:T]), hf[:, j, NM:T])
            n_hi += KC

            def gates_out(B, n, bufs=None):
                with act.Fori(0, KC) as i:
                    p0, p1, p2 = pos(B, 0, i), pos(B, 1, i), pos(B, 2, i)
                    begin(p0, p1)
                    act.wait_ge(evicted[p1[2]], p1[1])
                    nc.scalar.activation(row(gate[:, :], n), slot_ap(p0[2], n), ACT.Sigmoid)\
                        .then_inc(evicted[p0[2]], 1)
                    split_hi(*p2)

            def splits(B, count):
                with act.Fori(0, count // 2) as i:
                    for j in range(2):
                        split_hi(*pos(B, j + 1, i))

            def splits_one(B):
                split_hi(*pos(B, 1))

            def value_tiles(B, count, done):
                with act.Fori(0, count // 2) as i:
                    for j in range(2):
                        split_hi(*pos(B, j + 1, i))
                    for j in range(2):
                        act.wait_ge(vtr_done, done + 2 * i + j + 1)
                        cols_ = bass.ds(P * (2 * i + j), P)
                        nc.scalar.activation(vt[:, 1:5, cols_], ps[:, 6, :].rearrange("p (k v) -> p k v", k=4),
                                             ACT.Copy)
                        nc.scalar.activation(flat(vt[0:NM, 0:1, cols_]), ps[0:NM, 7, 0:P], ACT.Copy)\
                            .then_inc(vt_done, 1)

            gates_out(START["conv_out"], SEQ)

            splits(START["ret_qkv"], 8)
            value_tiles(START["ret_qkv"] + 8, 8, 0)
            for h in range(RH):
                act.wait_ge(ro_ready, h + 1)
                nc.scalar.activation(kk[:, 2 * h:2 * h + 2, NM:T], ps[:, 2 * (h % 2):2 * (h % 2) + 2, :],
                                     ACT.Copy).then_inc(ro_copied, 1)
            for h in range(RH):
                for v in range(2):
                    sum_squares(kk[:, 2 * h + v, NM:T], lambda: act.wait_ge(centred, 2 * h + v + 1))
            for h in range(RH):
                act.wait_ge(sq_used, n_sq - 2 * RH + 2 * h + 2)
                root(at[:, h, :], ps[:, h, :], 1.0 / RDV)
            B = START["ret_gate"]
            with act.Fori(0, KC // 2) as i:
                for j in range(2):
                    p0, p1 = pos(B, j, i), pos(B, j + 1, i)
                    begin(p0, p1)
                    act.wait_ge(hf_ready, n_hf + 2 * i + j)
                    nc.scalar.activation(gate[:, NM:T], slot_ap(p0[2], SEQ), ACT.Silu).then_inc(evicted[p0[2]], 1)
                    act.wait_ge(hf_ready, n_hf + 2 * i + j + 1)
                    hi_of(flat(bh[:, bass.ds(2 * i + j, 1), NM:T]), hf[:, j, NM:T])
            n_hf += KC
            n_hi += KC
            gates_out(START["ret_out"], SEQ)

            splits(START["diff_qkv"], 16)
            value_tiles(START["diff_qkv"] + 16, 8, 8)
            for u in range(4 * DH + 2):
                if u < 4 * DH:
                    h, b = divmod(u, 4)
                    L = NM + P * (b + 1)
                    act.wait_ge(dmax_ready, u + 1)
                    for m in range(2):
                        c = 8 + 2 * (u % 2) + m
                        if m == 0 and u >= 2:
                            act.wait_ge(da_ready, u - 1)
                        nc.scalar.activation(prob[u % 2][m][:, 0:L], prob[u % 2][m][:, 0:L], ACT.Exp,
                                             bias=stat[:, 4 + 2 * (u % 2) + m:5 + 2 * (u % 2) + m],
                                             scale=DHD ** -0.5, accum_out=stat[:, c:c + 1]).then_inc(dp_ready, 1)
                if u >= 2:
                    w = u - 2
                    h, b = divmod(w, 4)
                    act.wait_ge(dt_ready, w + 1)
                    if b == 0 and h:
                        act.wait_ge(do_ready, h)
                    nc.scalar.activation(at[:, 0:b + 1, P * b:P * b + P],
                                         ps[:, 0, 0:P * (b + 1)].rearrange("p (k q) -> p k q", q=P), ACT.Copy)
                    nc.scalar.activation(atm[0:NM, P * b:P * b + P], ps[0:NM, 1, 0:P], ACT.Copy)\
                        .then_inc(dt_copied, 1)
                    if b == 3:
                        act.wait_ge(do_ready, h + 1)
                        nc.scalar.activation(qq[:, h, NM:T], ps[:, 2 + h % 2, :], ACT.Copy).then_inc(do_copied, 1)
            for h in range(DH):
                sum_squares(qq[:, h, NM:T], lambda: act.wait_ge(do_copied, h + 1))
            for g in range(2):
                for h in range(4):
                    act.wait_ge(sq_used, n_sq - DH + 4 * g + h + 1)
                    if g and h == 0:
                        act.wait_ge(hf_ready, n_hf + 4)
                    root(at[:, h, :], ps[:, 4 * g + h, :], 1.0 / (2 * DHD))
                for h in range(4 * g, 4 * g + 4):
                    act.wait_ge(hf_ready, n_hf + h + 1)
                    hi_of(bh[:, h, NM:T], hf[:, h % 2, NM:T])
            n_hf += DH
            n_hi += DH
            act.dma_start(res[:], x_t).then_inc(res_in, 16)
            gates_out(START["diff_out"], SEQ)
            for c in range(KC):
                act.wait_ge(mrg_ready, c + 1)
                if c == 0:
                    act.wait_ge(mm_done, START["diff_out"] + 16)
                hi_of(xh[:, c, NM:T], mrg[:, c, NM:T])
            n_hi += KC
            splits(START["w_out"], 8)

            def added(c):
                n, half, slot = pos(START["w_out"], c)
                act.wait_ge(evicted[slot], half + 1)
            norm(res, SEQ, added)
            norm_hi(SEQ)
            n_hf += KC
            for g in range(4):
                B = START[f"ffn{g}up"]
                with act.Fori(0, KC // 2) as i:
                    for j in range(2):
                        p0, p1 = pos(B, j, i), pos(B, j + 1, i)
                        begin(p0, p1)
                        nc.scalar.activation(tmp[:, j, NM:T], slot_ap(p0[2], SEQ), ACT.Relu).then_inc(relu_ready, 1)
                        act.wait_ge(evicted[p0[2]], p0[1] + 1)
                        hi_of(flat(bh[:, bass.ds(2 * i + j, 1), NM:T]), hf[:, j, NM:T])
                n_hi += KC
                splits(START[f"ffn{g}down"], KC)
            def added(c):
                n, half, slot = pos(START["ffn3down"], c)
                act.wait_ge(evicted[slot], half + 1)
            norm(res, SEQ, added)

            act.dma_start(res[:, :, 0:NM], meta2_t).then_inc(meta_in, 16)
            act.dma_start(glm[:], gla_masks).then_inc(const2_in, 16)
            act.dma_start(lrw[:], wgk).then_inc(const2_in, 16)
            act.wait_ge(meta_in, 16)
            norm(res, T, lambda c: act.wait_ge(h_ready, c + 1))
            act.dma_start(res_dram, res[:]).then_inc(res_saved, 16)
            norm_hi(T)
            n_hf += KC
            splits(START["sb_qkv"], 8)
            value_tiles(START["sb_qkv"] + 8, 4, 16)
            act.wait_ge(res_saved, 16)
            for h in range(SH + 1):
                if h < SH:
                    k = h % 2
                    act.wait_ge(sz_ready, h + 1)
                    for dst, src in stick_pieces(h):
                        nc.scalar.activation(dst, src, ACT.Abs).then_inc(sabs_done, 1)
                    act.wait_ge(sabs_done, 4 * h + 4)
                    link(nc.scalar.activation(sbt[k], sbt[k], ACT.Exp, scale=-1.0))
                    link(nc.scalar.activation(sbm[k], sbm[k], ACT.Exp, scale=-1.0))
                    nc.scalar.activation(sbt[k], sbt[k], ACT.Ln, bias=1.0).then_inc(slog_done, 1)
                    nc.scalar.activation(sbm[k], sbm[k], ACT.Ln, bias=1.0).then_inc(slog_done, 1)
                if h:
                    w, k = h - 1, (h - 1) % 2
                    z = 4 * k
                    act.wait_ge(scum_done, w + 1)
                    for dst, src in stick_pieces(w):
                        nc.scalar.activation(dst, src, ACT.Exp).then_inc(sw_done, 1)
                    act.wait_ge(so_ready, w + 1)
                    f = slice(SHD * (w % 2), SHD * (w % 2) + SHD)
                    nc.scalar.activation(bh[f, w // 2, NM:T], ps[f, z, :], ACT.Copy)
                    nc.scalar.activation(bh[f, w // 2, 0:NM], ps[f, z + 3, 0:NM], ACT.Copy).then_inc(so_hi, 1)
            gates_out(START["sb_out"], T)

            splits_one(START["gla_lr"])
            for h in range(GH):
                act.wait_ge(gy_ready, h + 1)
                y = ps[:, 4 + 2 * (h % 2):6 + 2 * (h % 2), 0:HALF]
                if h >= 2:
                    act.wait_ge(glog_done, h - 1)
                link(nc.scalar.activation(two(grow[h % 2]), y, ACT.Abs, bias=wcol("b_gk_2", h)))
                act.wait_ge(gy_abs, h + 1)
                link(nc.scalar.activation(grow[h % 2], grow[h % 2], ACT.Exp, scale=-1.0))
                nc.scalar.activation(grow[h % 2], grow[h % 2], ACT.Ln, bias=1.0).then_inc(gy_log, 1)
            splits(START["gla_qkv"], 8)
            value_tiles(START["gla_qkv"] + 8, 8, 20)
            for h in range(GH):
                act.wait_ge(gcum_done, 2 * h + 1)
                if h:
                    act.wait_ge(go_ready, h)
                nc.scalar.activation(qc, cum, ACT.Exp, scale=1 / GATE_TAU)
                nc.scalar.activation(stat[:, 0:1], cum[:, NM - 1:NM], ACT.Exp, scale=1 / GATE_TAU)
                nc.scalar.activation(stat[:, 1:5], cum[:, NM + P - 1:T:P], ACT.Exp, scale=1 / GATE_TAU)\
                    .then_inc(gexp_done, 1)
                act.wait_ge(gcum_done, 2 * h + 2)
                nc.scalar.activation(kh, kh, ACT.Exp, scale=1 / GATE_TAU).then_inc(gexp_done, 1)
                for k, L, lo in levels():
                    act.wait_ge(gd_ready, 7 * h + k + 1)
                    nc.scalar.activation(grow[k % 2][:, lo:T], grow[k % 2][:, lo:T], ACT.Exp, scale=1 / GATE_TAU)\
                        .then_inc(ge_ready, 1)
                for c in range(4):
                    act.wait_ge(gt_ready, 4 * h + c + 1)
                    _, C = chunk(c)
                    nc.scalar.activation(ktok[c % 2][0:C, :], ps[0:C, 2, P:2 * P], ACT.Copy).then_inc(gt_copied, 1)
                act.wait_ge(go_ready, h + 1)
                o = otile(h, 0)
                nc.scalar.activation(kk[:, o:o + 2, NM:T], ps[:, 0:2, :], ACT.Copy)
                nc.scalar.activation(kk[:, o:o + 2, 0:NM], ps[:, 2, 0:2 * NM].rearrange("p (v t) -> p v t", v=2),
                                     ACT.Copy).then_inc(go_copied, 1)
            for h in range(GH):
                for v in range(2):
                    sum_squares(kk[:, otile(h, v), :], lambda: act.wait_ge(go_copied, GH))
                act.wait_ge(sq_used, n_sq)
                b = 4 + 2 * (h % 2)
                root(two(srow[h]), ps[:, b:b + 2, 0:HALF], 1.0 / GDV)
            B = START["gla_gate"]
            with act.Fori(0, KC // 2) as i:
                for j in range(2):
                    p0, p1 = pos(B, j, i), pos(B, j + 1, i)
                    begin(p0, p1)
                    act.wait_ge(hf_ready, n_hf + 2 * i + j)
                    nc.scalar.activation(two(gate[:, :]), slot_ap(p0[2], T), ACT.Silu).then_inc(evicted[p0[2]], 1)
                    act.wait_ge(hf_ready, n_hf + 2 * i + j + 1)
                    hi_of(flat(bh[:, bass.ds(2 * i + j, 1), :]), hf[:, j, :])
            n_hf += KC
            n_hi += KC
            act.dma_start(res[:], res_dram).then_inc(res_back, 16)
            gates_out(START["gla_out"], T)
            for c in range(KC):
                act.wait_ge(mrg_ready, KC + c + 1)
                if c == 0:
                    act.wait_ge(mm_done, START["gla_out"] + 16)
                hi_of(xh[:, c, :], mrg[:, c, :])
            n_hi += KC
            splits(START["w_o"], 8)
            def stored_mix(c):
                n, half, slot = pos(START["w_o"], c)
                act.wait_ge(evicted[slot], half + 1)
            norm(mrg, T, stored_mix)
            norm(res, T, lambda c: act.wait_ge(mix_added, c + 1))
            norm_hi(T)
            n_hf += KC
            tile = 0
            for g, n_g in enumerate(FFN2_GROUPS):
                B = START[f"glu{g}up"]
                with act.Fori(0, n_g // 2) as i:
                    for j in range(2):
                        up, gt, nx = pos(B, 2 * j, i, 4), pos(B, 2 * j + 1, i, 4), pos(B, 2 * j + 2, i, 4)
                        begin(up, gt)
                        nc.scalar.activation(two(tmp[:, j]), slot_ap(up[2], T), ACT.Copy).then_inc(evicted[up[2]], 1)
                        split_hi(*nx)
                        act.wait_ge(glu_copied, tile + 2 * i + j + 1)
                        nc.scalar.activation(gate[:, NM:T], hf[:, j, NM:T], ACT.Gelu_apprx_tanh).then_inc(glu_act, 1)
                        act.wait_ge(evicted[gt[2]], gt[1] + 1)
                        hi_of(flat(bh[:, bass.ds(2 * i + j, 1), NM:T]), hf[:, j, NM:T])
                tile += n_g
                n_hi += n_g
                splits(START[f"glu{g}down"], KC)
            def stored_ffn(c):
                n, half, slot = pos(START["glu2down"], c)
                act.wait_ge(evicted[slot], half + 1)
            norm(mrg, SEQ, stored_ffn)
            for c in range(0, KC, 2):
                act.wait_ge(out_ready, c + 2)
                act.dma_start(out[:, c:c + 2], mrg[:, c:c + 2, NM:T]).then_inc(stored, 16)
            act.wait_ge(stored, 64)

        @block.vector
        def _(dve):
            link = Link(dve, dve_self)
            n_hi = n_root = n_x = n_b = 0

            def split_lo(n, half, slot):
                dve.wait_ge(hi_done, n + 1)
                nc.vector.tensor_tensor(wl[:, slot], wraw[:, slot], wh[:, slot].bitcast(F32), ALU.subtract)\
                    .then_inc(lo_done, 1)

            def begin(this, next_one):
                split_lo(*next_one)
                dve.wait_ge(mm_done, this[0] + 1)

            def lo_of(dst, src, hi, ready, n):
                dve.wait_ge(hf_hi, n)
                nc.vector.tensor_tensor(dst, src, hi.bitcast(F32), ALU.subtract).then_inc(ready, 1)

            def invert(ap):
                nonlocal n_root
                n_root += 1
                dve.wait_ge(root_ready, n_root)
                link(nc.vector.reciprocal(ap, ap))

            def norm_apply(src, w, n):
                nonlocal n_hi, n_x
                invert(rsq[:, T - n:T])
                tok = slice(T - n, T)
                for c in range(KC + 1):
                    if c < KC:
                        if c >= 2:
                            dve.wait_ge(x_ready, n_x + c - 1)
                        nc.vector.scalar_tensor_tensor(out=hf[:, c % 2, tok], in0=src[:, c, tok], scalar=wcol(w, c),
                                                       in1=rsq[:, tok], op0=ALU.mult, op1=ALU.mult)\
                            .then_inc(hf_ready, 1)
                    if c:
                        d = c - 1
                        dve.wait_ge(hf_ready, n_hf + c)
                        lo_of(xl[:, d, tok], hf[:, d % 2, tok], xh[:, d, tok], x_ready, n_hi + d + 1)
                n_hi += KC
                n_x += KC

            link(nc.vector.memset(small[:], EPS))
            nc.vector.nop().then_inc(eps_set, 1)
            dve.wait_ge(params_in, 48)
            for k in range(2):
                if k:
                    dve.wait_ge(lam_sums, 1)
                a, b = lamr[:, 128 * k:128 * k + 64], lamr[:, 128 * k + 64:128 * k + 128]
                nc.vector.tensor_tensor_reduce(out=a, in0=a, in1=b, scale=1.0, scalar=0.0, op0=ALU.mult, op1=ALU.add,
                                               accum_out=small[:, 1 + k:2 + k]).then_inc(lam_sums, 1)
            dve.wait_ge(lam_exps, 1)
            link(nc.vector.tensor_tensor(small[:, 5:6], small[:, 4:5], small[:, 3:4], ALU.subtract))
            link(nc.vector.tensor_scalar(small[:, 5:6], small[:, 5:6], -LAM_INIT, None, ALU.add))
            link(nc.vector.tensor_scalar(wcol("diff_subln_w"), wcol("diff_subln_w"), 1.0 - LAM_INIT, None, ALU.mult))
            n_hf = 0

            norm_apply(res, "norm1_w", T)
            n_hf += KC
            split_lo(0, 0, 0)

            B = START["conv_in"]
            o = COLS["conv_w"][0]
            with link.loop(KC // 2, 2 * 3) as i:
                for j in range(2):
                    p = [pos(B, 3 * j + k, i, 6) for k in range(4)]
                    split_lo(*p[1])
                    begin(p[1], p[2])
                    dve.wait_ge(evicted[p[0][2]], p[0][1] + 1)
                    nc.vector.tensor_tensor(two(tmp[:, j]), slot_ap(p[1][2], T), two(gate[:, :]), ALU.mult)\
                        .then_inc(evicted[p[1][2]], 1)
                    dve.wait_ge(evicted[p[1][2]], p[1][1] + 1)
                    taps = [col[:, bass.ds(3 * (2 * i + j) + (o + k), 1)] for k in range(3)]
                    y = hf[:, j, NM:T]
                    link(nc.vector.tensor_scalar(y, tmp[:, j, NM - 2:T - 2], taps[0], None, ALU.mult))
                    for k in (1, 2):
                        link(nc.vector.scalar_tensor_tensor(out=y, in0=tmp[:, j, NM - 2 + k:T - 2 + k],
                                                            scalar=taps[k], in1=y, op0=ALU.mult, op1=ALU.add))
                    begin(p[2], p[3])
                    nc.vector.tensor_tensor(y, slot_ap(p[2][2], SEQ), y, ALU.mult).then_inc(evicted[p[2][2]], 1)
                    lo_of(flat(bl[:, bass.ds(2 * i + j, 1), NM:T]), y, flat(bh[:, bass.ds(2 * i + j, 1), NM:T]),
                          b_ready, n_hi + 2 * i + j + 1)
            n_hi += KC

            def branch_out(B, n, first, last=False):
                with dve.Fori(0, KC) as i:
                    p0, p1, p2 = pos(B, 0, i), pos(B, 1, i), pos(B, 2, i)
                    split_lo(*p1)
                    begin(p1, p2)
                    dve.wait_ge(evicted[p0[2]], p0[1] + 1)
                    m = flat(mrg[:, bass.ds(i, 1), T - n:T])
                    m = m if n == SEQ else two(m)
                    dst = m if first else row(tmp[:, 0], n)
                    nc.vector.tensor_tensor(dst, slot_ap(p1[2], n), row(gate[:, :], n), ALU.mult)\
                        .then_inc(evicted[p1[2]], 1)
                    if not first:
                        dve.wait_ge(evicted[p1[2]], p1[1] + 1)
                        nc.vector.tensor_tensor(m, m, row(tmp[:, 0], n), ALU.add).then_inc(mrg_ready if last else mrg_sum, 1)

            def store(B, count, dst, scale=None, n=T):
                with dve.Fori(0, count // 2) as i:
                    for j in range(2):
                        p0 = pos(B, j, i)
                        begin(p0, pos(B, j + 1, i))
                        d = flat(dst[:, bass.ds(2 * i + j, 1), :])
                        if scale is None:
                            ins = nc.vector.tensor_copy(two(d), slot_ap(p0[2], T))
                        else:
                            ins = nc.vector.tensor_scalar(two(d), slot_ap(p0[2], T), scale, None, ALU.mult)
                        ins.then_inc(evicted[p0[2]], 1)

            def store_values(B, count, done):
                with dve.Fori(0, count // 2) as i:
                    for j in range(2):
                        p0 = pos(B, j, i)
                        begin(p0, pos(B, j + 1, i))
                        dve.wait_ge(vtr_done, 2 * i + done)
                        nc.vector.tensor_copy(two(tmp[:, j]), slot_ap(p0[2], T)).then_inc(evicted[p0[2]], 1)

            branch_out(START["conv_out"], SEQ, True)

            B = START["ret_qkv"]
            store(B, 4, qq[:, 0:4])
            store(B + 4, 4, qq[:, 4:8], P ** -0.5)
            store_values(B + 8, 8, 0)
            n_mask = 0
            for h in range(RH):
                dve.wait_ge(table_in[h % 2], 16 * (h // 2 + 1))
                if h:
                    dve.wait_ge(ro_ready, h)
                for t, q0 in key_tiles():
                    dve.wait_ge(rz_ready, 4 * h + min(t, 3) + 1)
                    if t == 0:
                        o_, s_, m_ = atm[0:NM, :], ps[0:NM, 4, :], tbl[h % 2][0:NM, NM:T]
                    else:
                        L = SEQ - q0
                        s_ = ps[:, 4 + t, 0:L] if t < 4 else ps[:, 7, 256:256 + L]
                        o_, m_ = at[:, t - 1, q0:SEQ], tbl[h % 2][:, 0:L]
                    nc.vector.tensor_tensor(o_, s_, m_, ALU.mult).then_inc(rs_masked, 1)
            for h in range(RH):
                dve.wait_ge(mean_ready, h + 1)
                for v in range(2):
                    y = kk[:, 2 * h + v, NM:T]
                    nc.vector.scalar_tensor_tensor(out=y, in0=ps[:, 4 + h, :], scalar=-1.0 / RDV, in1=y,
                                                   op0=ALU.mult, op1=ALU.add).then_inc(centred, 1)
            dve.wait_ge(centred, 2 * RH)
            for h in range(RH):
                invert(at[:, h, :])
                for v in range(2):
                    y = kk[:, 2 * h + v, NM:T]
                    link(nc.vector.tensor_tensor(y, y, at[:, h, :], ALU.mult))
            B = START["ret_gate"]
            with dve.Fori(0, KC // 2) as i:
                for j in range(2):
                    p0 = pos(B, j, i)
                    begin(p0, pos(B, j + 1, i))
                    dve.wait_ge(evicted[p0[2]], p0[1] + 1)
                    c = bass.ds(2 * i + j, 1)
                    nc.vector.tensor_tensor(hf[:, j, NM:T], gate[:, NM:T], flat(kk[:, c, NM:T]), ALU.mult)\
                        .then_inc(hf_ready, 1)
                    dve.wait_ge(hf_ready, n_hf + 2 * i + j + 1)
                    lo_of(flat(bl[:, c, NM:T]), hf[:, j, NM:T], flat(bh[:, c, NM:T]), b_ready, n_hi + 2 * i + j + 1)
            n_hf += KC
            n_hi += KC
            branch_out(START["ret_out"], SEQ, False)

            B = START["diff_qkv"]
            store(B, 8, qq)
            store(B + 8, 8, kk)
            store_values(B + 16, 8, 8)
            for u in range(4 * DH + 1):
                if u < 4 * DH:
                    h, b = divmod(u, 4)
                    L, j0 = NM + P * (b + 1), P * (3 - b)
                    if b == 0:
                        dve.wait_ge(table_in[h % 2], 32 + 16 * (h // 2 + 1))
                    if u >= 2:
                        dve.wait_ge(da_ready, u - 1)
                    for m in range(2):
                        c = 2 * (u % 2) + m
                        dve.wait_ge(dz_ready, 2 * u + m + 1)
                        src = ps[:, 4 + 2 * m:6 + 2 * m, :].rearrange("p b q -> p (b q)")[:, 0:L]
                        nc.vector.tensor_tensor_reduce(
                            out=prob[u % 2][m][:, 0:L], in0=src, in1=tbl[h % 2][:, j0:T], scale=1.0, scalar=-3e38,
                            op0=ALU.add, op1=ALU.max, accum_out=stat[:, c:c + 1]).then_inc(ds_ready, 1)
                    dve.wait_ge(ds_ready, 2 * u + 2)
                    c = 2 * (u % 2)
                    nc.vector.tensor_scalar(stat[:, 4 + c:6 + c], stat[:, c:c + 2], -DHD ** -0.5, None,
                                            ALU.mult).then_inc(dmax_ready, 1)
                if u:
                    w = u - 1
                    h, b = divmod(w, 4)
                    L = NM + P * (b + 1)
                    p1, p2 = (prob[w % 2][m][:, 0:L] for m in range(2))
                    c = 8 + 2 * (w % 2)
                    dve.wait_ge(dp_ready, 2 * w + 2)
                    link(nc.vector.reciprocal(stat[:, c + 4:c + 6], stat[:, c:c + 2]))
                    link(nc.vector.tensor_tensor(stat[:, c + 5:c + 6], stat[:, c + 5:c + 6], small[:, 5:6], ALU.mult))
                    link(nc.vector.tensor_scalar(p2, p2, stat[:, c + 5:c + 6], None, ALU.mult))
                    if w >= 2:
                        dve.wait_ge(dt_ready, w - 1)
                    nc.vector.scalar_tensor_tensor(out=tmp[:, w % 2, 0:L], in0=p1, scalar=stat[:, c + 4:c + 5],
                                                   in1=p2, op0=ALU.mult, op1=ALU.add).then_inc(da_ready, 1)
            for h in range(DH + 1):
                if h < DH:
                    invert(at[:, h % 4, :])
                    nc.vector.scalar_tensor_tensor(out=hf[:, h % 2, NM:T], in0=qq[:, h, NM:T],
                                                   scalar=wcol("diff_subln_w"), in1=at[:, h % 4, :],
                                                   op0=ALU.mult, op1=ALU.mult).then_inc(hf_ready, 1)
                if h:
                    d = h - 1
                    dve.wait_ge(hf_ready, n_hf + h)
                    lo_of(bl[:, d, NM:T], hf[:, d % 2, NM:T], bh[:, d, NM:T], b_ready, n_hi + d + 1)
            n_hf += DH
            n_hi += DH
            branch_out(START["diff_out"], SEQ, False, True)
            for c in range(KC):
                lo_of(xl[:, c, NM:T], mrg[:, c, NM:T], xh[:, c, NM:T], x_ready, n_hi + c + 1)
            n_hi += KC
            n_x += KC

            def accumulate(B, n=SEQ):
                with dve.Fori(0, KC // 2) as i:
                    for j in range(2):
                        p0 = pos(B, j, i)
                        begin(p0, pos(B, j + 1, i))
                        r = flat(res[:, bass.ds(2 * i + j, 1), T - n:T])
                        nc.vector.tensor_tensor(r, slot_ap(p0[2], n), r, ALU.add).then_inc(evicted[p0[2]], 1)

            dve.wait_ge(res_in, 16)
            accumulate(START["w_out"])
            norm_apply(res, "norm2_w", SEQ)
            n_hf += KC
            for g in range(4):
                B = START[f"ffn{g}up"]
                with dve.Fori(0, KC // 2) as i:
                    for j in range(2):
                        p0 = pos(B, j, i)
                        begin(p0, pos(B, j + 1, i))
                        dve.wait_ge(relu_ready, KC * g + 2 * i + j + 1)
                        dve.wait_ge(b_ready, (3 + g) * KC + 2 * i + j - 1)
                        nc.vector.scalar_tensor_tensor(out=hf[:, j, NM:T], in0=slot_ap(p0[2], SEQ), scalar=0.0,
                                                       in1=tmp[:, j, NM:T], op0=ALU.max, op1=ALU.mult)\
                            .then_inc(evicted[p0[2]], 1)
                        c = bass.ds(2 * i + j, 1)
                        lo_of(flat(bl[:, c, NM:T]), hf[:, j, NM:T], flat(bh[:, c, NM:T]), b_ready,
                              n_hi + 2 * i + j + 1)
                n_hi += KC
                accumulate(START[f"ffn{g}down"])
            invert(rsq[:, NM:T])
            for c in range(KC):
                y = res[:, c, NM:T]
                nc.vector.scalar_tensor_tensor(out=y, in0=y, scalar=wcol("final_norm_w", c), in1=rsq[:, NM:T],
                                               op0=ALU.mult, op1=ALU.mult).then_inc(h_ready, 1)

            norm_apply(res, "norm_mix_pre_2", T)
            n_hf += KC
            B = START["sb_qkv"]
            store(B, 4, qq[:, 0:4], SHD ** -0.5)
            store(B + 4, 4, qq[:, 4:8])
            store_values(B + 8, 4, 16)
            for h in range(SH + 1):
                if h < SH:
                    k, z = h % 2, 4 * (h % 2)
                    dve.wait_ge(slog_done, 2 * h + 2)
                    for dst, src in stick_pieces(h):
                        nc.vector.scalar_tensor_tensor(out=dst, in0=src, scalar=0.0, in1=dst, op0=ALU.max,
                                                       op1=ALU.add).then_inc(sp_done, 1)
                if h:
                    w = h - 1
                    z = 4 * (w % 2)
                    f = slice(SHD * (w % 2), SHD * (w % 2) + SHD)
                    dve.wait_ge(so_hi, w + 1)
                    nc.vector.tensor_tensor(bl[f, w // 2, NM:T], ps[f, z, :], bh[f, w // 2, NM:T].bitcast(F32),
                                            ALU.subtract)
                    nc.vector.tensor_tensor(bl[f, w // 2, 0:NM], ps[f, z + 3, 0:NM],
                                            bh[f, w // 2, 0:NM].bitcast(F32), ALU.subtract).then_inc(b_ready, 1)
            branch_out(START["sb_out"], T, True)

            p0 = pos(START["gla_lr"])
            begin(p0, pos(START["gla_lr"], 1))
            nc.vector.tensor_copy(two(tmp[0:NM, 0]), ps[0:NM, 2 * p0[2]:2 * p0[2] + 2, 0:HALF])\
                .then_inc(evicted[p0[2]], 1)
            dve.wait_ge(const2_in, 32)
            for h in range(GH):
                dve.wait_ge(gy_ready, h + 1)
                y = ps[:, 4 + 2 * (h % 2):6 + 2 * (h % 2), 0:HALF]
                dve.wait_ge(act_self, 2 * SH + 2 * h + 1)
                nc.vector.tensor_scalar(two(kk[:, h, :]), y, wcol("b_gk_2", h), 0.0, ALU.add, ALU.min)\
                    .then_inc(gy_abs, 1)
                dve.wait_ge(gy_log, h + 1)
                dve.wait_ge(gy_abs, h + 1)
                nc.vector.tensor_tensor(kk[:, h, :], kk[:, h, :], grow[h % 2], ALU.subtract).then_inc(glog_done, 1)
            B = START["gla_qkv"]
            store(B, 4, qq[:, 0:4], P ** -0.5)
            store(B + 4, 4, qq[:, 4:8])
            store_values(B + 8, 8, 20)
            link(nc.vector.memset(gtmp, 1.0))
            link(nc.vector.memset(gtmp[:, 0:1], 0.0))
            link(nc.vector.memset(gtmp[:, NM:T:P], 0.0))
            for h in range(GH):
                q, k_ = qq[:, h, :], qq[:, 4 + h, :]
                if h:
                    dve.wait_ge(go_ready, h)
                nc.vector.tensor_tensor_scan(cum, gtmp, kk[:, h, :], 0.0, ALU.mult, ALU.add).then_inc(gcum_done, 1)
                dve.wait_ge(gcum_done, 2 * h + 1)
                link(nc.vector.tensor_tensor(kh[:, 0:NM], cum[:, NM - 1:NM].to_broadcast([P, NM]), cum[:, 0:NM],
                                             ALU.subtract))
                c3, k3 = (r[:, NM:T].rearrange("p (c t) -> p c t", c=4) for r in (cum, kh))
                nc.vector.tensor_tensor(k3, c3[:, :, P - 1:P].to_broadcast([P, 4, P]), c3, ALU.subtract)\
                    .then_inc(gcum_done, 1)

                def distances(k, L, lo):
                    d, s_ = halves(grow[k % 2], L, lo), halves(cum, L, lo)
                    n = (T - lo) // (2 * L)
                    mid = s_[:, :, 0, L - 1:L].to_broadcast([P, n, L])
                    nc.vector.tensor_tensor(d[:, :, 0, :], mid, s_[:, :, 0, :], ALU.subtract)
                    nc.vector.tensor_tensor(d[:, :, 1, :], s_[:, :, 1, :], mid, ALU.subtract).then_inc(gd_ready, 1)

                def factors(k, L, lo):
                    x, e = halves(xl_rows[k], L, lo), halves(grow[k % 2], L, lo)
                    dve.wait_ge(ge_ready, 7 * h + k + 1)
                    nc.vector.tensor_tensor(x[:, :, 0, :], halves(k_, L, lo)[:, :, 0, :], e[:, :, 0, :], ALU.mult)
                    nc.vector.tensor_tensor(x[:, :, 1, :], halves(q, L, lo)[:, :, 1, :], e[:, :, 1, :], ALU.mult)\
                        .then_inc(gx_ready, 1)

                lv = levels()
                distances(*lv[0])
                distances(*lv[1])
                dve.wait_ge(gexp_done, 2 * h + 2)
                link(nc.vector.tensor_tensor(qc, qc, q, ALU.mult))
                link(nc.vector.tensor_tensor(kh, kh, k_, ALU.mult))
                for k in range(7):
                    factors(*lv[k])
                    if k + 2 < 7:
                        dve.wait_ge(gx_ready, 7 * h + k + 1)
                        distances(*lv[k + 2])
                for c in range(5):
                    u = 5 * h + c
                    _, C = chunk(c)
                    l0 = 3 if c == 0 else 0
                    dve.wait_ge(gp_ready, u + 1)
                    if u:
                        dve.wait_ge(ga_ready, u)
                    b = 4 + 2 * (c % 2)
                    src = ps[0:C, b:b + 2, :].rearrange("p b (l t) -> p (b l) t", t=P)[:, l0:8, 0:C]
                    nc.vector.tensor_tensor(masked[0:C, l0:8, 0:C], src, glm[0:C, l0:8, 0:C], ALU.mult)\
                        .then_inc(gp_used, 1)
                    dve.wait_ge(gp_used, u + 1)
                    if c >= 2:
                        dve.wait_ge(gs_ready, 4 * h + c - 1)
                    nc.vector.tensor_reduce(amat[c % 2][0:C, 0:C],
                                            masked[0:C, l0:8, 0:C].rearrange("p l t -> p t l"), AX, ALU.add)\
                        .then_inc(ga_ready, 1)
                    if c < 4:
                        dve.wait_ge(gs_ready, 4 * h + c + 1)
                    if c == 0:
                        nc.vector.tensor_copy(state[0], ps[:, 3, 0:GDV]).then_inc(gs_done, 1)
                    elif c < 4:
                        dve.wait_ge(gs_done, 4 * h + c)
                        nc.vector.scalar_tensor_tensor(out=state[c % 2], in0=state[(c - 1) % 2],
                                                       scalar=stat[:, c:c + 1], in1=ps[:, 3, 0:GDV], op0=ALU.mult,
                                                       op1=ALU.add).then_inc(gs_done, 1)
            for h in range(GH):
                invert(srow[h])
                for v in range(2):
                    o = kk[:, otile(h, v), :]
                    link(nc.vector.scalar_tensor_tensor(out=o, in0=o, scalar=wcol("gla_head_norm_2", v),
                                                        in1=srow[h], op0=ALU.mult, op1=ALU.mult))
            B = START["gla_gate"]
            with dve.Fori(0, KC // 2) as i:
                for j in range(2):
                    p0 = pos(B, j, i)
                    begin(p0, pos(B, j + 1, i))
                    dve.wait_ge(evicted[p0[2]], p0[1] + 1)
                    c = bass.ds(2 * i + j, 1)
                    nc.vector.tensor_tensor(hf[:, j, :], gate[:, :], flat(kk[:, c, :]),
                                            ALU.mult).then_inc(hf_ready, 1)
                    dve.wait_ge(hf_ready, n_hf + 2 * i + j + 1)
                    lo_of(flat(bl[:, c, :]), hf[:, j, :], flat(bh[:, c, :]), b_ready, n_hi + 2 * i + j + 1)
            n_hf += KC
            n_hi += KC
            branch_out(START["gla_out"], T, False, True)
            for c in range(KC):
                lo_of(xl[:, c, :], mrg[:, c, :], xh[:, c, :], x_ready, n_hi + c + 1)
            n_hi += KC
            n_x += KC
            dve.wait_ge(x_ready, n_x)
            store(START["w_o"], 8, mrg)
            invert(rsq[:, :])
            dve.wait_ge(res_back, 16)
            for c in range(KC):
                link(nc.vector.scalar_tensor_tensor(out=mrg[:, c, :], in0=mrg[:, c, :],
                                                    scalar=wcol("norm_mix_post_2", c), in1=rsq[:, :],
                                                    op0=ALU.mult, op1=ALU.mult))
                nc.vector.tensor_tensor(res[:, c, :], res[:, c, :], mrg[:, c, :], ALU.add).then_inc(mix_added, 1)
            norm_apply(res, "norm_ffn_pre_2", T)
            n_hf += KC
            tile = 0
            for g, n_g in enumerate(FFN2_GROUPS):
                B = START[f"glu{g}up"]
                oc, ob = COLS["conv_w_2"][0] + 3 * tile, COLS["conv_b_2"][0] + tile
                with link.loop(n_g // 2, 4) as i:
                    for j in range(2):
                        up, gt, nx = pos(B, 2 * j, i, 4), pos(B, 2 * j + 1, i, 4), pos(B, 2 * j + 2, i, 4)
                        split_lo(*gt)
                        dve.wait_ge(evicted[up[2]], up[1] + 1)
                        taps = [col[:, bass.ds(3 * (2 * i + j) + (oc + k), 1)] for k in range(3)]
                        y = hf[:, j, NM:T]
                        dve.wait_ge(b_ready, 8 * KC + SH + tile + 2 * i + j - 1)
                        link(nc.vector.tensor_scalar(y, tmp[:, j, NM - 2:T - 2], taps[0],
                                                     col[:, bass.ds(2 * i + (ob + j), 1)], ALU.mult, ALU.add))
                        for k in (1, 2):
                            ins = nc.vector.scalar_tensor_tensor(out=y, in0=tmp[:, j, NM - 2 + k:T - 2 + k],
                                                                 scalar=taps[k], in1=y, op0=ALU.mult, op1=ALU.add)
                            if k == 1:
                                link(ins)
                            else:
                                ins.then_inc(glu_copied, 1)
                        begin(gt, nx)
                        dve.wait_ge(glu_act, tile + 2 * i + j + 1)
                        nc.vector.tensor_tensor(y, slot_ap(gt[2], SEQ), gate[:, NM:T], ALU.mult)\
                            .then_inc(evicted[gt[2]], 1)
                        c = bass.ds(2 * i + j, 1)
                        lo_of(flat(bl[:, c, NM:T]), y, flat(bh[:, c, NM:T]), b_ready, n_hi + 2 * i + j + 1)
                tile += n_g
                n_hi += n_g
                B = START[f"glu{g}down"]
                with dve.Fori(0, KC // 2) as i:
                    for j in range(2):
                        p0 = pos(B, j, i)
                        begin(p0, pos(B, j + 1, i))
                        m = flat(mrg[:, bass.ds(2 * i + j, 1), NM:T])
                        if g == 0:
                            ins = nc.vector.tensor_copy(m, slot_ap(p0[2], SEQ))
                        else:
                            ins = nc.vector.tensor_tensor(m, slot_ap(p0[2], SEQ), m, ALU.add)
                        ins.then_inc(evicted[p0[2]], 1)
            invert(rsq[:, NM:T])
            for c in range(KC):
                m = mrg[:, c, NM:T]
                link(nc.vector.scalar_tensor_tensor(out=m, in0=m, scalar=wcol("norm_ffn_post_2", c),
                                                    in1=rsq[:, NM:T], op0=ALU.mult, op1=ALU.mult))
                nc.vector.tensor_tensor(m, m, res[:, c, NM:T], ALU.add).then_inc(out_ready, 1)

        @block.tensor
        def _(pe):
            n_sq = n_x = n_b = 0

            def strip(p, src, n, chunks=range(KC), dst=None, ready=None, wchunk=lambda c: c):
                number, half, slot = p
                hi, lo = (xh, xl) if src == "x" else (bh, bl)
                pe.wait_ge(lo_done, number + 1)
                if not (isinstance(half, int) and half == 0):
                    pe.wait_ge(evicted[slot], half)
                rows = [(slice(NM, T), ps[:, 2 * slot, :])] if n == SEQ else \
                    [(slice(HALF * k, HALF * k + HALF), ps[:, 2 * slot + k, 0:HALF]) for k in range(2)]
                for c in chunks:
                    if ready is not None:
                        pe.wait_ge(ready[0], ready[1] + c + 1)
                    for w, a in ((wh, hi), (wh, lo), (wl, hi)):
                        for tok, o in rows:
                            last = nc.tensor.matmul(o, w[:, slot, wchunk(c), :], a[:, c, tok],
                                                    start=(c == chunks[0] and w is wh and a is hi),
                                                    stop=(c == chunks[-1] and w is wl))
                last.then_inc(mm_done, 1)

            def strips(B, count, src, n, ready=None, peel=True):
                lo = 0
                if ready is not None:
                    for j in range(2):
                        strip(pos(B, j), src, n, ready=ready if j == 0 else None)
                    lo = 1
                with pe.Fori(lo, count // 2) as i:
                    for j in range(2):
                        strip(pos(B, j, i), src, n)

            def sum_rows(bank, rows, n=SEQ, squares=True):
                nonlocal n_sq
                for k in range(rows):
                    pe.wait_ge(sq_ready, n_sq + 1)
                    for tok, o in ([(slice(NM, T), ps[:, bank, :])] if n == SEQ else
                                   [(slice(HALF * q, HALF * q + HALF), ps[:, bank + q, 0:HALF]) for q in range(2)]):
                        last = nc.tensor.matmul(o, ones, tmp[:, n_sq % 2, tok], start=(k == 0), stop=(k == rows - 1))
                    last.then_inc(sq_used, 1)
                    n_sq += 1

            def value_strips(B, count, done):
                with pe.Fori(0, count // 2) as i:
                    for j in range(2):
                        strip(pos(B, j, i), "x", T)
                    for j in range(2):
                        p0 = pos(B, j, i)
                        pe.wait_ge(evicted[p0[2]], p0[1] + 1)
                        pe.wait_ge(vt_done, done + 2 * i + j)
                        for kb in range(4):
                            nc.tensor.transpose(ps[:, 6, P * kb:P * kb + P], tmp[:, j, NM + P * kb:NM + P * kb + P],
                                                ident)
                        nc.tensor.transpose(ps[0:NM, 7, 0:P], tmp[:, j, 0:NM], ident).then_inc(vtr_done, 1)

            pe.wait_ge(params_in, 48)
            sum_rows(4, KC, T)
            B = START["conv_in"]
            for k in range(6):
                strip(pos(B, k), "x", SEQ if k % 3 == 2 else T, ready=(x_ready, 0) if k == 0 else None)
            with pe.Fori(1, KC // 2) as i:
                for k in range(6):
                    strip(pos(B, k, i, 6), "x", SEQ if k % 3 == 2 else T)
            n_x = KC

            def branch_strips(B, n, readyb):
                strip(pos(B, 0), "x", n)
                strip(pos(B, 1), "b", n, ready=(b_ready, readyb))
                with pe.Fori(1, KC) as i:
                    strip(pos(B, 0, i), "x", n)
                    strip(pos(B, 1, i), "b", n)

            branch_strips(START["conv_out"], SEQ, 0)
            strips(START["ret_qkv"], 8, "x", T)
            value_strips(START["ret_qkv"] + 8, 8, 0)
            def scores(h):
                for t, q0 in key_tiles():
                    if h and t < 4:
                        pe.wait_ge(rs_masked, 5 * (h - 1) + (t + 1 if t < 3 else 5))
                    keys = qq[:, 4 + h, 0:NM] if t == 0 else qq[:, 4 + h, NM + q0:NM + q0 + P]
                    L = SEQ - q0
                    o = ps[0:NM, 4, :] if t == 0 else ps[:, 4 + t, 0:L] if t < 4 else ps[:, 7, 256:256 + L]
                    ins = nc.tensor.matmul(o, keys, qq[:, h, NM + q0:T], start=True, stop=True)
                    if t != 3:
                        ins.then_inc(rz_ready, 1)

            def products(h):
                pe.wait_ge(rs_masked, 5 * h + 5)
                if h >= 2:
                    pe.wait_ge(ro_copied, h - 1)
                for v in range(2):
                    f = RDV * h + P * v
                    for t, q0 in key_tiles():
                        o = ps[:, 2 * (h % 2) + v, q0:SEQ]
                        if t == 0:
                            nc.tensor.matmul(o, vt[0:NM, 0, f:f + P], atm[0:NM, :], start=True, stop=False)
                        else:
                            ins = nc.tensor.matmul(o, vt[:, t, f:f + P], at[:, t - 1, q0:SEQ], start=False,
                                                   stop=(t == 4))
                ins.then_inc(ro_ready, 1)

            pe.wait_ge(vt_done, 8)
            scores(0)
            for h in range(RH):
                if h + 1 < RH:
                    scores(h + 1)
                products(h)
            for h in range(RH):
                pe.wait_ge(ro_copied, h + 1)
                for v in range(2):
                    ins = nc.tensor.matmul(ps[:, 4 + h, :], ones, kk[:, 2 * h + v, NM:T], start=(v == 0),
                                           stop=(v == 1))
                ins.then_inc(mean_ready, 1)
            for h in range(RH):
                sum_rows(h, 2)
            pe.wait_ge(root_ready, 1 + RH)
            strips(START["ret_gate"], KC, "x", SEQ)
            branch_strips(START["ret_out"], SEQ, KC)
            strips(START["diff_qkv"], 16, "x", T)
            value_strips(START["diff_qkv"] + 16, 8, 8)
            pe.wait_ge(vt_done, 16)
            for u in range(4 * DH + 2):
                if u < 4 * DH:
                    h, b = divmod(u, 4)
                    L = NM + P * (b + 1)
                    for m in range(2):
                        if u:
                            pe.wait_ge(ds_ready, 2 * u - 1 + m)
                        f = slice(DHD * m, DHD * m + DHD)
                        q = qq[f, h, NM + P * b:NM + P * b + P]
                        for lo, hi in ((0, min(L, SEQ)), (SEQ, L)):
                            if lo < hi:
                                ins = nc.tensor.matmul(ps[:, 4 + 2 * m + lo // SEQ, 0:hi - lo], q, kk[f, h, lo:hi],
                                                       start=True, stop=True)
                        ins.then_inc(dz_ready, 1)
                if u >= 2:
                    w = u - 2
                    h, b = divmod(w, 4)
                    pe.wait_ge(da_ready, w + 1)
                    if w:
                        pe.wait_ge(dt_copied, w)
                    a = tmp[:, w % 2]
                    for kb in range(b + 1):
                        nc.tensor.transpose(ps[:, 0, P * kb:P * kb + P], a[:, NM + P * kb:NM + P * kb + P], ident)
                    nc.tensor.transpose(ps[0:NM, 1, 0:P], a[:, 0:NM], ident).then_inc(dt_ready, 1)
                    if b == 3:
                        pe.wait_ge(dt_copied, w + 1)
                        if h >= 2:
                            pe.wait_ge(do_copied, h - 1)
                        for t, q0 in key_tiles():
                            o = ps[:, 2 + h % 2, q0:SEQ]
                            if t == 0:
                                nc.tensor.matmul(o, vt[0:NM, 0, P * h:P * h + P], atm[0:NM, :], start=True,
                                                 stop=False)
                            else:
                                ins = nc.tensor.matmul(o, vt[:, t, P * h:P * h + P], at[:, t - 1, q0:SEQ],
                                                       start=False, stop=(t == 4))
                        ins.then_inc(do_ready, 1)
            pe.wait_ge(do_copied, DH)
            for h in range(DH):
                sum_rows(h, 1)
            pe.wait_ge(root_ready, 1 + RH + 8)
            branch_strips(START["diff_out"], SEQ, 2 * KC)
            strips(START["w_out"], 8, "x", SEQ, ready=(x_ready, KC))
            sum_rows(4, KC, SEQ)
            for g in range(4):
                strips(START[f"ffn{g}up"], KC, "x", SEQ, ready=(x_ready, 2 * KC) if g == 0 else None)
                strips(START[f"ffn{g}down"], KC, "b", SEQ, ready=(b_ready, (3 + g) * KC))
            sum_rows(4, KC, SEQ)

            sum_rows(4, KC, T)
            strips(START["sb_qkv"], 8, "x", T, ready=(x_ready, 3 * KC))
            value_strips(START["sb_qkv"] + 8, 4, 16)
            def logits(h):
                z, f = 4 * (h % 2), slice(SHD * (h % 2), SHD * (h % 2) + SHD)
                q, k = qq[f, h // 2], qq[f, 4 + h // 2]
                if h >= 2:
                    pe.wait_ge(b_ready, 7 * KC + h - 1)
                nc.tensor.matmul(ps[0:NM, z, :], k[:, 0:NM], q[:, NM:T], start=True, stop=True)
                for t in range(4):
                    o, L = sb_bank(z, t)
                    nc.tensor.matmul(o, k[:, NM + P * t:NM + P * t + P], q[:, NM + P * t:T], start=(t < 3),
                                     stop=True, skip_group_check=True)
                    last = nc.tensor.matmul(o[:, 0:P], identb[:], negm[:], start=False, stop=True,
                                            skip_group_check=True)
                o = ps[0:NM, z + 3, 384:384 + NM]
                nc.tensor.matmul(o, k[:, 0:NM], q[:, 0:NM], start=False, stop=True, skip_group_check=True)
                nc.tensor.matmul(o, identb[0:NM, 0:NM], negm[0:NM, 0:NM], start=False, stop=True,
                                 skip_group_check=True).then_inc(sz_ready, 1)

            def sb_bank(z, t):
                L = SEQ - P * t
                return (ps[:, z + 1 + t, 0:L], L) if t < 3 else (ps[:, z + 3, 256:256 + L], L)

            def subtract_sums(h):
                k, z = h % 2, 4 * (h % 2)
                pe.wait_ge(sp_done, 4 * h + 4)
                for t in range(4):
                    o, L = sb_bank(z, t)
                    for t2 in range(t, 4):
                        L2 = SEQ - P * t2
                        nc.tensor.matmul(o[:, L - L2:L], ntri if t2 == t else nones, sbt[k][:, SB0[t2]:SB0[t2] + L2],
                                         start=False, stop=(t2 == 3), skip_group_check=True)
                o = ps[0:NM, z, :]
                for t2 in range(4):
                    L2 = SEQ - P * t2
                    nc.tensor.matmul(o[:, SEQ - L2:SEQ], nones[:, 0:NM], sbt[k][:, SB0[t2]:SB0[t2] + L2],
                                     start=False, stop=False, skip_group_check=True)
                nc.tensor.matmul(o, ntri[0:NM, 0:NM], sbm[k][:, NM:T], start=False, stop=True,
                                 skip_group_check=True)
                nc.tensor.matmul(ps[0:NM, z + 3, 384:384 + NM], ntri[0:NM, 0:NM], sbm[k][:, 0:NM], start=False,
                                 stop=True, skip_group_check=True).then_inc(scum_done, 1)

            def sb_products(h):
                k, z, f = h % 2, 4 * (h % 2), slice(SHD * (h % 2), SHD * (h % 2) + SHD)
                v = slice(SHD * h, SHD * h + SHD)
                pe.wait_ge(sw_done, 4 * h + 4)
                nc.tensor.matmul(ps[f, z, :], vt[0:NM, 0, v], sbm[k][:, NM:T], start=True, stop=False)
                for t in range(4):
                    L = SEQ - P * t
                    nc.tensor.matmul(ps[f, z, P * t:SEQ], vt[:, 1 + t, v], sbt[k][:, SB0[t]:SB0[t] + L],
                                     start=False, stop=(t == 3))
                nc.tensor.matmul(ps[f, z + 3, 0:NM], vt[0:NM, 0, v], sbm[k][:, 0:NM], start=True, stop=True)\
                    .then_inc(so_ready, 1)

            pe.wait_ge(vt_done, 20)
            pe.wait_ge(masks_made, 1)
            logits(0)
            logits(1)
            for h in range(SH):
                subtract_sums(h)
                sb_products(h)
                if h + 2 < SH:
                    logits(h + 2)
            pe.wait_ge(b_ready, 7 * KC + SH)
            with pe.Fori(0, KC) as i:
                strip(pos(START["sb_out"], 0, i), "x", T)
                strip(pos(START["sb_out"], 1, i), "b", T, chunks=range(4))
            p0 = pos(START["gla_lr"])
            strip(p0, "x", T)
            pe.wait_ge(evicted[p0[2]], p0[1] + 1)
            pe.wait_ge(const2_in, 32)
            for h in range(GH):
                if h >= 2:
                    pe.wait_ge(gy_abs, h - 1)
                for k in range(2):
                    ins = nc.tensor.matmul(ps[:, 4 + 2 * (h % 2) + k, 0:HALF], lrw[:, P * h:P * h + P],
                                           tmp[0:NM, 0, HALF * k:HALF * k + HALF], start=True, stop=True)
                ins.then_inc(gy_ready, 1)
            strips(START["gla_qkv"], 8, "x", T)
            value_strips(START["gla_qkv"] + 8, 8, 20)
            pe.wait_ge(vt_done, 28)

            def level_products(h, c):
                tok, C = chunk(c)
                u = 5 * h + c
                if c == 0:
                    pe.wait_ge(gx_ready, 7 * h + 7)
                if u >= 2:
                    pe.wait_ge(gp_used, u - 1)
                for k, L, lo in levels():
                    if L < C:
                        x = xl_rows[k][:, tok]
                        nc.tensor.matmul(ps[0:C, 4 + 2 * (c % 2) + k // 4, P * (k % 4):P * (k % 4) + C], x, x,
                                         start=True, stop=True)
                nc.tensor.matmul(ps[0:C, 5 + 2 * (c % 2), 3 * P:3 * P + C], qq[:, 4 + h, tok], qq[:, h, tok],
                                 start=True, stop=True).then_inc(gp_ready, 1)

            for h in range(GH):
                level_products(h, 0)
                for c in range(5):
                    tok, C = chunk(c)
                    u = 5 * h + c
                    if c < 4:
                        level_products(h, c + 1)
                        if c:
                            pe.wait_ge(gt_copied, 4 * h + c)
                        elif h:
                            pe.wait_ge(go_copied, h)
                        nc.tensor.transpose(ps[0:C, 2, P:2 * P], kh[:, tok], ident).then_inc(gt_ready, 1)
                    pe.wait_ge(ga_ready, u + 1)
                    if c:
                        pe.wait_ge(gs_done, 4 * h + c)
                    else:
                        pe.wait_ge(gt_copied, 4 * h + 1)
                    for v in range(2):
                        f = GDV * h + P * v
                        o = ps[:, 2, NM * v:NM * v + NM] if c == 0 else ps[:, v, P * (c - 1):P * c]
                        ins = nc.tensor.matmul(o, vt[0:C, c, f:f + P], amat[c % 2][0:C, 0:C], start=True,
                                               stop=(c == 0))
                        if c:
                            ins = nc.tensor.matmul(o, state[(c - 1) % 2][:, P * v:P * v + P], qc[:, tok],
                                                   start=False, stop=True)
                    if c < 4:
                        pe.wait_ge(gt_copied, 4 * h + c + 1)
                        nc.tensor.matmul(ps[:, 3, 0:GDV], ktok[c % 2][0:C, :], vt[0:C, c, GDV * h:GDV * h + GDV],
                                         start=True, stop=True).then_inc(gs_ready, 1)
                    else:
                        ins.then_inc(go_ready, 1)
            for h in range(GH):
                if h >= 2:
                    pe.wait_ge(root_ready, N_ROOTS + h - 1)
                sum_rows(4 + 2 * (h % 2), 2, T)
            strips(START["gla_gate"], KC, "x", T)
            strip(pos(START["gla_out"], 0), "x", T)
            strip(pos(START["gla_out"], 1), "b", T, ready=(b_ready, 7 * KC + SH))
            with pe.Fori(1, KC) as i:
                strip(pos(START["gla_out"], 0, i), "x", T)
                strip(pos(START["gla_out"], 1, i), "b", T)
            strips(START["w_o"], 8, "x", T, ready=(x_ready, 4 * KC))
            sum_rows(4, KC, T)
            pe.wait_ge(root_ready, N_ROOTS + GH + 1)
            sum_rows(4, KC, T)
            done = 8 * KC + SH
            for g, n_g in enumerate(FFN2_GROUPS):
                B = START[f"glu{g}up"]
                for k in range(4):
                    strip(pos(B, k), "x", SEQ if k % 2 else T, ready=(x_ready, 5 * KC) if g == k == 0 else None)
                with pe.Fori(1, n_g // 2) as i:
                    for k in range(4):
                        strip(pos(B, k, i, 4), "x", SEQ if k % 2 else T)
                B = START[f"glu{g}down"]
                strip(pos(B, 0), "b", SEQ, chunks=range(n_g), ready=(b_ready, done))
                strip(pos(B, 1), "b", SEQ, chunks=range(n_g))
                with pe.Fori(1, KC // 2) as i:
                    for j in range(2):
                        strip(pos(B, j, i), "b", SEQ, chunks=range(n_g))
                done += n_g
            sum_rows(4, KC, SEQ)

        @block.gpsimd
        def _(pool):
            for h in range(RH + DH):
                if h == 0:
                    pool.wait_ge(b_ready, KC)
                elif h == RH:
                    pool.wait_ge(b_ready, 2 * KC)
                elif 1 < h < RH:
                    pool.wait_ge(rs_masked, 5 * (h - 1))
                elif h > RH + 1:
                    pool.wait_ge(ds_ready, 8 * (h - RH - 1))
                pool.dma_start(tbl[h % 2], tables[h]).then_inc(table_in[h % 2], 16)
            nc.gpsimd.memset(negm[:], 0.0).then_inc(pool_self, 1)
            pool.wait_ge(pool_self, 1)
            nc.gpsimd.affine_select(out=negm[:], in_=negm[:], compare_op=ALU.is_gt, fill=-1e30, base=0,
                                    pattern=[[1, P]], channel_multiplier=-1).then_inc(pool_self, 1)
            pool.wait_ge(params_in, 48)
            pool.wait_ge(pool_self, 2)
            nc.gpsimd.tensor_copy(identb[:], ident).then_inc(masks_made, 1)



def feature_tiles(a):
    return np.ascontiguousarray(a.reshape(-1, P, a.shape[-1]).transpose(1, 0, 2))


def strips_of(w, cols):
    return [w[:, c:c + P].reshape(-1, P, P).transpose(1, 0, 2) for c in cols]


def weight_strips(a):
    w = a["w_in"][0]
    rq, rk, rv, rg, dq, dk, dv, cb, cc, cx, gates = (0, 512, 1024, 2048, 3072, 4096, 5120, 6144, 7168, 8192, 9216)
    s = []

    def tiles(w, first, n):
        return strips_of(w, range(first, first + P * n, P))

    def woven(*lists):
        return [x for group in zip(*lists) for x in group]

    s += woven(tiles(w, cc, 8), tiles(w, cx, 8), tiles(w, cb, 8))
    s += woven(tiles(w, gates + 2 * D, 8), tiles(a["w_branch"][0, 2], 0, 8))
    s += tiles(w, rq, 4) + tiles(w, rk, 4) + tiles(w, rv, 8) + tiles(w, rg, 8)
    s += woven(tiles(w, gates, 8), tiles(a["w_branch"][0, 0], 0, 8))
    s += tiles(w, dq, 8) + tiles(w, dk, 8) + tiles(w, dv, 8)
    s += woven(tiles(w, gates + D, 8), tiles(a["w_branch"][0, 1], 0, 8))
    s += tiles(a["w_out"][0], 0, 8)
    for g in range(4):
        s += tiles(a["w_up"][0], g * D, 8) + tiles(a["w_down"][0][g * D:g * D + D], 0, 8)
    s += second_strips(a, tiles, woven)
    s.append(np.zeros((P, KC, P), np.float32))
    out = np.empty((len(s), P, KC, P), np.float32)
    for i, x in enumerate(s):
        out[i, :, :x.shape[1]] = x
        out[i, :, x.shape[1]:] = 0
    return out


def second_strips(a, tiles, woven):
    w = a["w_in_2"][0]
    sq, sk, sv, gq, gk, gv, gr, lr, mg = (0, 512, 1024, 1536, 2048, 2560, 3584, 4608, 4624)
    s = tiles(w, sq, 4) + tiles(w, sk, 4) + tiles(w, sv, 4)
    s += woven(tiles(w, mg, 8), tiles(a["w_sb_out_2"][0], 0, 8))
    low = np.zeros((D, P), np.float32)
    low[:, :NM] = w[:, lr:lr + NM]
    s += tiles(low, 0, 1) + tiles(w, gq, 4) + tiles(w, gk, 4) + tiles(w, gv, 8)
    s += tiles(w, gr + 4 * P, 4) + tiles(w, gr, 4)
    s += woven(tiles(w, mg + D, 8), [np.roll(x, 4, axis=1) for x in tiles(a["w_gla_out_2"][0], 0, 8)])
    s += tiles(a["w_o_2"][0], 0, 8)
    first = 0
    for n in FFN2_GROUPS:
        s += woven(tiles(a["w_ffn_up_2"][0], first, n), tiles(a["w_ffn_gate_2"][0], first, n))
        s += tiles(a["w_ffn_down_2"][0][first:first + P * n], 0, 8)
        first += P * n
    return s


def gla_level_masks():
    s, t = np.arange(P)[:, None], np.arange(P)[None, :]
    m = [(s // (2 * L) == t // (2 * L)) & (s & L == 0) & (t & L != 0) for L in (64, 32, 16, 8, 4, 2, 1)]
    return np.ascontiguousarray(np.stack(m + [s == t]).astype(np.float32).transpose(1, 0, 2))


def shape_tables():
    j, p = np.arange(T)[None, :], np.arange(P)[:, None]
    log_g = np.log1p(-np.exp2(-5.0 - np.arange(RH)))
    decay = [np.where(j >= p, np.exp(g * np.maximum(j - p, 0)), 0.0) for g in log_g]
    dist = p + 3 * P + NM - j
    slopes = np.exp2(-8.0 / DH * (np.arange(DH) + 1.0))
    alibi = [np.where(dist >= 0, -s * DHD ** 0.5 * dist, -1e30) for s in slopes]
    return np.stack(decay + alibi).astype(np.float32)


def shape_consts():
    i, j = np.arange(P)[:, None], np.arange(P)[None, :]
    return np.ascontiguousarray(np.stack([i == j, i >= 0 * j, -(i >= j).astype(int), -(i >= 0 * j).astype(int)]).astype(
        np.float32).transpose(1, 0, 2))


def columns(a):
    c = []
    for name, (_, n) in COLS.items():
        v = a[name]
        if name == "conv_w":
            c.append(v[0].reshape(3, KC, P).transpose(2, 1, 0).reshape(P, -1))
        elif name == "conv_w_2":
            c.append(v[0].reshape(3, FT2, P).transpose(2, 1, 0).reshape(P, -1))
        else:
            c.append(v.reshape(n, P).T)
    return np.ascontiguousarray(np.concatenate(c, axis=1))


def device_inputs(a):
    return {
        "weights": weight_strips(a),
        "cols": columns(a),
        "tables": shape_tables(),
        "consts": shape_consts(),
        "lam_rows": np.ascontiguousarray(np.broadcast_to(a["diff_lambda"].reshape(1, -1), (P, 4 * DHD))),
        "x_t": feature_tiles(np.concatenate([a["meta_tokens"], a["x"][0]], axis=0).T),
        "meta2_t": feature_tiles(np.ascontiguousarray(a["meta_tokens_2"].T)),
        "gla_masks": gla_level_masks(),
        "wgk": np.ascontiguousarray(a["w_gk_up_2"][0]),
    }


def kernel(**inputs):
    import concourse.bacc as bacc
    from concourse.bass_utils import run_bass_kernel_spmd

    arrays = device_inputs({k: np.asarray(v) for k, v in inputs.items()})
    nc = bacc.Bacc("TRN2", target_bir_lowering=False, num_devices=1)
    args = {n: nc.dram_tensor(f"{n}_dram", v.shape, F32, kind="ExternalInput").ap() for n, v in arrays.items()}
    res_dram = nc.dram_tensor("res_dram", [P, KC, T], F32).ap()
    out = nc.dram_tensor("out_dram", [P, KC, SEQ], F32, kind="ExternalOutput").ap()
    build(nc, res_dram=res_dram, out=out, **args)
    r = run_bass_kernel_spmd(nc, [{f"{n}_dram": v for n, v in arrays.items()}], core_ids=[0])
    got = r.results[0]["out_dram"]
    return np.ascontiguousarray(got.transpose(2, 1, 0).reshape(1, SEQ, D))
```

```python
from contextlib import ExitStack, contextmanager

import numpy as np

import concourse.bass as bass
from concourse import mybir

F32 = mybir.dt.float32
F32R = mybir.dt.float32r
BF16 = mybir.dt.bfloat16
ALU = mybir.AluOpType
ACT = mybir.ActivationFunctionType
AX = mybir.AxisListType.X

P = 128
D = 1024
KC = D // P
NM = 16
SEQ = 512
T = NM + SEQ
HALF = T // 2
EPS = 1e-6
RH, RDV = 4, 256
DH, DHD = 8, 64
LAM_INIT = 0.2
FF1 = 4 * D
SH, SHD = 8, 64
GH, GDV = 4, 256
GATE_TAU = 16.0
FF2 = 2816
FT2 = FF2 // P

SIGMOID, LN_EXP, GELU, SILU = 2, 6, 11, 18

COLS = {}
for _name, _n in (("norm1_w", 8), ("norm2_w", 8), ("final_norm_w", 8), ("diff_subln_w", 1), ("conv_w", 24),
                  ("norm_mix_pre_2", 8), ("gla_head_norm_2", 2), ("norm_mix_post_2", 8), ("norm_ffn_pre_2", 8),
                  ("norm_ffn_post_2", 8), ("conv_w_2", 3 * FT2), ("conv_b_2", FT2), ("b_gk_2", 4)):
    COLS[_name] = (sum(n for _, n in COLS.values()), _n)
NCOL = sum(n for _, n in COLS.values())

FFN2_GROUPS = (8, 8, 6)
PHASES = [("conv_in", 24), ("conv_out", 16), ("ret_qkv", 16), ("ret_gate", 8), ("ret_out", 16), ("diff_qkv", 24),
          ("diff_out", 16), ("w_out", 8)]
PHASES += [(f"ffn{g}{s}", 8) for g in range(4) for s in ("up", "down")]
PHASES += [("sb_qkv", 12), ("sb_out", 16), ("gla_lr", 1), ("gla_qkv", 16), ("gla_gate", 8), ("gla_out", 16),
           ("w_o", 8)]
for _g, _n in enumerate(FFN2_GROUPS):
    PHASES += [(f"glu{_g}up", 2 * _n), (f"glu{_g}down", 8)]
START = {}
for _name, _n in PHASES:
    START[_name] = sum(p[1] for p in PHASES[:len(START)])
NSTRIP = sum(p[1] for p in PHASES)


def pos(base, k=0, i=0, step=2):
    return base + k + step * i, (base + k) // 2 + (step // 2) * i, (base + k) % 2


def flat(ap):
    return ap.rearrange("p a t -> p (a t)")


class Link:

    def __init__(self, eng, sem):
        self.eng, self.sem, self.base, self.n = eng, sem, 0, 0

    def __call__(self, ins):
        ins.then_inc(self.sem, 1)
        self.n += 1
        self.eng.wait_ge(self.sem, self.base + self.n)

    @contextmanager
    def loop(self, count, per):
        before = self.base + self.n
        with self.eng.Fori(0, count) as i:
            self.base, self.n = before + i * per, 0
            yield i
            assert self.n == per, (self.n, per)
        self.base, self.n = before + count * per, 0


def first_then_loop(eng, count, body):
    body(0)
    with eng.Fori(1, count) as i:
        body(i)


def two(ap):
    return ap.rearrange("p (h t) -> p h t", h=2)


def build(nc, weights, cols, tables, consts, lam_rows, x_t, meta2_t, wgk, gla_masks, res_dram, mrg_dram,
          out):
    ctx = ExitStack()
    with ctx:
        def sb(name, shape, dt=F32):
            return ctx.enter_context(nc.sbuf_tensor(name, shape, dt))

        def sem(name):
            return ctx.enter_context(nc.semaphore(name))

        xh, xl = sb("xh", [P, KC, T], F32R), sb("xl", [P, KC, T], F32R)
        bh, bl = sb("bh", [P, KC, T], F32R), sb("bl", [P, KC, T], F32R)
        wraw = sb("wraw", [P, 2, KC, P])
        wh, wl = sb("wh", [P, 2, KC, P], F32R), sb("wl", [P, 2, KC, P], F32R)
        qq, kk = sb("qq", [P, KC, T]), sb("kk", [P, KC, T])
        vt = sb("vt", [P, 5, D])
        mrg = sb("mrg", [P, KC, T])
        res = sb("res", [P, KC, T])
        tmp = sb("tmp", [P, 2, T])
        hf = sb("hf", [P, 2, T])
        gate = sb("gate", [P, T])
        rsq = gate
        cst = sb("cst", [P, 4, P])
        ident, ones, ntri, nones = (cst[:, i, :] for i in range(4))
        col = sb("col", [P, NCOL])
        small = sb("small", [P, 8])
        stat = sb("stat", [P, 16])
        xrows = sb("xrows", [P, 5, T])
        glm = sb("glm", [P, 8, P])
        negm = sb("negm", [P, P], BF16)
        identb = sb("identb", [P, P], BF16)
        lrw = sb("lrw", [NM, 4 * P])
        lamr = sb("lamr", [P, 4 * DHD])
        ps = ctx.enter_context(nc.psum_tensor("ps", [P, 8, 512], F32))

        scr = res[:, :, :].rearrange("p c t -> p (c t)")
        SBW = 4 * P + 3 * P + 2 * P + P
        sbt = [scr[:, (SBW + T) * k:(SBW + T) * k + SBW] for k in range(2)]
        sbm = [scr[0:NM, (SBW + T) * k + SBW:(SBW + T) * (k + 1)] for k in range(2)]
        SB0 = (0, 512, 896, 1152)
        srow = [res[:, k, :] for k in range(8)]
        xl_rows = ([xrows[:, k, :] for k in range(5)] + srow[0:2], [mrg[:, k, :] for k in range(7)])
        cums = (srow[2], mrg[:, 7, :])
        qcs = (srow[3], kk[:, 6, :], srow[3], qq[:, 0, :])
        khs = (srow[4], kk[:, 7, :], srow[4], qq[:, 4, :])
        grow, gtmp = (srow[5], srow[6]), srow[7]
        masked = hf[:, :, :].rearrange("p a t -> p (a t)")[:, 0:8 * P].rearrange("p (l t) -> p l t", l=8)
        amat = [tmp[:, 0, P * k:P * k + P] for k in range(2)]
        ktok = [tmp[:, 1, P * k:P * k + P] for k in range(2)]
        state = [gate[:, GDV * k:GDV * k + GDV] for k in range(2)]
        at = scr[:, 0:2048].rearrange("p (k q) -> p k q", k=4)
        atm = scr[:, 2048:2560]
        prob = [[scr[:, 2560 + T * m:2560 + T * (m + 1)] for m in range(2)],
                [scr[:, 2560 + 2 * T:2560 + 3 * T], gate[:, :]]]
        tbl = [hf[:, 0, :], hf[:, 1, :]]

        def wcol(name, i=0):
            o = COLS[name][0] + i
            return col[:, o:o + 1] if isinstance(i, int) else col[:, bass.ds(o, 1)]

        w_loaded = [sem("w_loaded0"), sem("w_loaded1")]
        hi_done, lo_done = sem("hi_done"), sem("lo_done")
        mm_done = sem("mm_done")
        evicted = [sem("evicted0"), sem("evicted1")]
        x_ready, b_ready = sem("x_ready"), sem("b_ready")
        act_self, dve_self = sem("act_self"), sem("dve_self")
        params_in, x_in, table_in, res_in = sem("params_in"), sem("x_in"), sem("table_in"), sem("res_in")
        table_in = [sem("table_in0"), sem("table_in1")]
        sq_ready, sq_used = sem("sq_ready"), sem("sq_used")
        sq_added = sem("sq_added")
        ln_done, root_ready = sem("ln_done"), sem("root_ready")
        hf_ready, hf_hi = sem("hf_ready"), sem("hf_hi")
        relu_ready = sem("relu_ready")
        vtr_done, vt_done = sem("vtr_done"), sem("vt_done")
        lam_sums, lam_exps, eps_set = sem("lam_sums"), sem("lam_exps"), sem("eps_set")
        rz_ready, rs_masked, ro_ready, ro_copied = (sem(n) for n in ("rz_ready", "rs_masked", "ro_ready", "ro_copied"))
        mean_ready, centred, r_scaled = sem("mean_ready"), sem("centred"), sem("r_scaled")
        dz_ready, ds_ready, dmax_ready, dp_ready, da_ready, dt_ready, dt_copied, do_ready, do_squared, do_summed, do_scaled = (
            sem(n) for n in ("dz_ready", "ds_ready", "dmax_ready", "dp_ready", "da_ready", "dt_ready", "dt_copied",
                             "do_ready", "do_squared", "do_summed",
                             "do_scaled"))
        mrg_ready, mrg_sum = sem("mrg_ready"), sem("mrg_sum")
        stored = sem("stored")
        h_ready, meta_in, res_saved, res_back, mrg_saved, mrg_back = (sem(n) for n in (
            "h_ready", "meta_in", "res_saved", "res_back", "mrg_saved", "mrg_back"))
        const2_in, masks_made, pool_self = sem("const2_in"), sem("masks_made"), sem("pool_self")
        sz_ready, sabs_done, slog_done, sp_done, scum_done, sw_done, so_ready, so_hi = (sem(n) for n in (
            "sz_ready", "sabs_done", "slog_done", "sp_done", "scum_done", "sw_done", "so_ready", "so_hi"))
        lr_ready, gy_ready, gy_abs, gy_log, glog_done = (sem(n) for n in (
            "lr_ready", "gy_ready", "gy_abs", "gy_log", "glog_done"))
        gcum_done, gexp_done, gd_ready, ge_ready, gx_ready = (sem(n) for n in (
            "gcum_done", "gexp_done", "gd_ready", "ge_ready", "gx_ready"))
        gp_ready, gp_used, ga_ready, gt_ready, gt_copied, gs_ready, gs_done, go_ready, go_copied = (sem(n) for n in (
            "gp_ready", "gp_used", "ga_ready", "gt_ready", "gt_copied", "gs_ready", "gs_done", "go_ready",
            "go_copied"))
        mix_added, glu_copied, glu_act, out_ready = (sem(n) for n in ("mix_added", "glu_copied", "glu_act",
                                                                      "out_ready"))

        def slot_ap(slot, n):
            return ps[:, 2 * slot, :] if n == SEQ else ps[:, 2 * slot:2 * slot + 2, 0:HALF]

        def row(ap, n):
            return ap[:, NM:T] if n == SEQ else two(ap)

        def key_tiles():
            return [(0, 0)] + [(kb + 1, P * kb) for kb in range(4)]

        def stick_pieces(h):
            k, z = h % 2, 4 * (h % 2)
            return ((sbt[k][:, 0:512], ps[:, z + 1, :]),
                    (sbt[k][:, 512:SBW].rearrange("p (b q) -> p b q", b=2), ps[:, z + 2:z + 4, 0:384]),
                    (sbm[k][:, NM:T], ps[0:NM, z, :]),
                    (sbm[k][:, 0:NM], ps[0:NM, z + 3, 384:384 + NM]))

        def otile(h, v):
            return (4 + 2 * h + v) % 8

        def levels():
            return [(k, L, 0 if L <= NM // 2 else NM) for k, L in enumerate((64, 32, 16, 8, 4, 2, 1))]

        def halves(r, L, lo):
            return r[:, lo:T].rearrange("p (n s l) -> p n s l", s=2, l=L)

        def chunk(c):
            return (slice(0, NM), NM) if c == 0 else (slice(NM + P * (c - 1), NM + P * c), P)

        n_strips = NSTRIP + 1

        N_ROOTS = 1 + RH + DH + 3
        block = ctx.enter_context(nc.Block())

        @block.sync
        def _(sp):
            def load(n, slot):
                sp.dma_start(wraw[:, slot], weights[bass.ds(n, 1)].rearrange("a p k n -> p (a k) n"))\
                    .then_inc(w_loaded[slot], 16)

            for n in range(2):
                load(n, n)
            with sp.Fori(1, n_strips // 2) as i:
                for k in range(2):
                    sp.wait_ge(lo_done, 2 * i + k - 1)
                    load(2 * i + k, k)
            if n_strips % 2:
                sp.wait_ge(lo_done, n_strips - 2)
                load(n_strips - 1, 0)

        @block.scalar
        def _(act):
            link = Link(act, act_self)
            n_hi = n_sq = n_root = n_added = 0

            def table_set(number):
                act.add_instruction(mybir.InstLoadActFuncSet(name=nc.get_next_instruction_name(),
                                                             engine=mybir.EngineType.Activation,
                                                             act_func_set_id=number))

            def split_hi(n, half, slot):
                act.wait_ge(w_loaded[slot], 16 * half + 16)
                if not (isinstance(n, int) and n < 2):
                    act.wait_ge(mm_done, n - 1)
                nc.scalar.activation(wh[:, slot], wraw[:, slot], ACT.Copy).then_inc(hi_done, 1)

            def begin(n_half_slot, next_one):
                split_hi(*next_one)
                act.wait_ge(mm_done, n_half_slot[0] + 1)

            def hi_of(dst, src):
                nc.scalar.activation(dst, src, ACT.Copy).then_inc(hf_hi, 1)

            def sum_squares(src, wait):
                nonlocal n_sq
                wait()
                if n_sq >= 2:
                    act.wait_ge(sq_used, n_sq - 1)
                tok = slice(T - src.shape[-1], T)
                nc.scalar.activation(tmp[:, n_sq % 2, tok], src, ACT.Square).then_inc(sq_ready, 1)
                n_sq += 1

            def root(dst, src, scale):
                nonlocal n_root
                n_root += 1
                nc.scalar.activation(dst, src, ACT.Ln, bias=small[:, 0:1], scale=scale).then_inc(ln_done, 1)
                act.wait_ge(ln_done, n_root)
                nc.scalar.activation(dst, dst, ACT.Exp, scale=-0.5).then_inc(root_ready, 1)

            def norm(src, n, wait=lambda c: None):
                for c in range(KC):
                    sum_squares(src[:, c, T - n:T], lambda: wait(c))
                act.wait_ge(sq_used, n_sq)
                root(row(rsq, n), ps[:, 4, :] if n == SEQ else ps[:, 4:6, 0:HALF], 1.0 / D)

            def norm_hi(n):
                nonlocal n_hi
                for c in range(KC):
                    act.wait_ge(hf_ready, n_hf + c + 1)
                    hi_of(xh[:, c, T - n:T], hf[:, c % 2, T - n:T])
                n_hi += KC

            act.dma_start(cst[:], consts).then_inc(params_in, 16)
            act.dma_start(col[:], cols).then_inc(params_in, 16)
            act.dma_start(lamr[:], lam_rows).then_inc(params_in, 16)
            for g in range(2):
                act.dma_start(res[:, 4 * g:4 * g + 4], x_t[:, 4 * g:4 * g + 4]).then_inc(x_in, 16)
            table_set(LN_EXP)
            act.wait_ge(lam_sums, 2)
            nc.scalar.activation(small[:, 3:5], small[:, 1:3], ACT.Exp).then_inc(lam_exps, 1)
            act.wait_ge(x_in, 32)
            act.wait_ge(eps_set, 1)
            n_hf = 0

            norm(res, T)
            split_hi(0, 0, 0)
            norm_hi(T)
            n_hf += KC

            B = START["conv_in"]
            def conv_strips(i):
                for j in range(2):
                    n, half, slot = pos(B, 3 * j, i, 6)
                    begin((n,), pos(B, 3 * j + 1, i, 6))
                    _, half1, slot1 = pos(B, 3 * j - 2, i, 6)
                    if not (isinstance(i, int) and j == 0):
                        act.wait_ge(evicted[slot1], half1 + 1)
                    nc.scalar.activation(two(gate[:, :]), slot_ap(slot, T), ACT.Copy).then_inc(evicted[slot], 1)
                    split_hi(*pos(B, 3 * j + 2, i, 6))
                    split_hi(*pos(B, 3 * j + 3, i, 6))
                    n2, half2, slot2 = pos(B, 3 * j + 2, i, 6)
                    act.wait_ge(evicted[slot2], half2 + 1)
                    hi_of(flat(bh[:, bass.ds(2 * i + j, 1), NM:T]), hf[:, j, NM:T])

            first_then_loop(act, KC // 2, conv_strips)
            n_hi += KC

            def gates_out(B, n, bufs=None):
                table_set(SIGMOID)
                with act.Fori(0, KC) as i:
                    p0, p1, p2 = pos(B, 0, i), pos(B, 1, i), pos(B, 2, i)
                    begin(p0, p1)
                    act.wait_ge(evicted[p1[2]], p1[1])
                    nc.scalar.activation(row(gate[:, :], n), slot_ap(p0[2], n), ACT.Sigmoid)\
                        .then_inc(evicted[p0[2]], 1)
                    split_hi(*p2)
                table_set(LN_EXP)

            def splits(B, count):
                with act.Fori(0, count // 2) as i:
                    for j in range(2):
                        split_hi(*pos(B, j + 1, i))

            def splits_and_root(B, src, n):
                nonlocal n_sq, n_added
                tok = slice(T - n, T)
                split_hi(*pos(B, 1))
                split_hi(*pos(B, 2))
                for c in range(KC):
                    _, half, slot = pos(B, c)
                    act.wait_ge(evicted[slot], half + 1)
                    if c == 0:
                        act.wait_ge(sq_used, n_sq)
                    if c >= 3:
                        act.wait_ge(sq_added, n_added + c - 2)
                    nc.scalar.activation(tmp[:, c % 2, tok] if c else hf[:, 0, tok], src[:, c, tok], ACT.Square)\
                        .then_inc(sq_ready, 1)
                    if c + 2 < KC:
                        split_hi(*pos(B, c + 3))
                n_sq += KC
                n_added += KC - 2
                act.wait_ge(sq_used, n_sq)
                root(row(rsq, n), ps[:, 4, :] if n == SEQ else ps[:, 4:6, 0:HALF], 1.0 / D)

            def splits_one(B):
                split_hi(*pos(B, 1))

            def value_tiles(B, count, done):
                def take(n):
                    act.wait_ge(vtr_done, n + (done + 1))
                    cols_ = bass.ds(P * n, P)
                    nc.scalar.activation(vt[:, 1:5, cols_], ps[:, 6, :].rearrange("p (k v) -> p k v", k=4), ACT.Copy)
                    nc.scalar.activation(flat(vt[0:NM, 0:1, cols_]), ps[0:NM, 7, 0:P], ACT.Copy).then_inc(vt_done, 1)

                split_hi(*pos(B, 1))
                split_hi(*pos(B, 2))
                with act.Fori(1, count // 2) as i:
                    for j in range(2):
                        take(2 * i + (j - 2))
                        split_hi(*pos(B, j + 1, i))
                take(count - 2)
                take(count - 1)

            gates_out(START["conv_out"], SEQ)

            splits(START["ret_qkv"], 8)
            value_tiles(START["ret_qkv"] + 8, 8, 0)
            for h in range(RH + 1):
                if h < RH:
                    act.wait_ge(ro_ready, h + 1)
                    nc.scalar.activation(kk[:, 2 * h:2 * h + 2, NM:T], ps[:, 2 * (h % 2):2 * (h % 2) + 2, :],
                                         ACT.Copy).then_inc(ro_copied, 1)
                if h:
                    w = h - 1
                    for v in range(2):
                        sum_squares(kk[:, 2 * w + v, NM:T], lambda: act.wait_ge(centred, 2 * w + v + 1))
                    act.wait_ge(sq_used, n_sq)
                    root(qq[:, w, NM:T], ps[:, 2 * (w % 2) + 1, :], 1.0 / RDV)
            B = START["ret_gate"]
            table_set(SILU)
            with act.Fori(0, KC // 2) as i:
                for j in range(2):
                    p0, p1 = pos(B, j, i), pos(B, j + 1, i)
                    begin(p0, p1)
                    act.wait_ge(hf_ready, n_hf + 2 * i + j)
                    nc.scalar.activation(gate[:, NM:T], slot_ap(p0[2], SEQ), ACT.Silu).then_inc(evicted[p0[2]], 1)
                    act.wait_ge(hf_ready, n_hf + 2 * i + j + 1)
                    hi_of(flat(bh[:, bass.ds(2 * i + j, 1), NM:T]), hf[:, j, NM:T])
            n_hf += KC
            n_hi += KC
            gates_out(START["ret_out"], SEQ)

            splits(START["diff_qkv"], 16)
            value_tiles(START["diff_qkv"] + 16, 8, 8)
            for u in range(4 * DH + 6):
                if u < 4 * DH:
                    h, b = divmod(u, 4)
                    L = NM + P * (b + 1)
                    act.wait_ge(dmax_ready, u + 1)
                    for m in range(2):
                        c = 8 + 2 * (u % 2) + m
                        if m == 0 and u >= 2:
                            act.wait_ge(da_ready, u - 1)
                        nc.scalar.activation(prob[u % 2][m][:, 0:L], prob[u % 2][m][:, 0:L], ACT.Exp,
                                             bias=stat[:, 4 + 2 * (u % 2) + m:5 + 2 * (u % 2) + m],
                                             scale=DHD ** -0.5, accum_out=stat[:, c:c + 1]).then_inc(dp_ready, 1)
                if 2 <= u < 4 * DH + 2:
                    w = u - 2
                    h, b = divmod(w, 4)
                    act.wait_ge(dt_ready, w + 1)
                    if b == 0 and h:
                        act.wait_ge(do_ready, h)
                    nc.scalar.activation(at[:, 0:b + 1, P * b:P * b + P],
                                         ps[:, 0, 0:P * (b + 1)].rearrange("p (k q) -> p k q", q=P), ACT.Copy)
                    nc.scalar.activation(atm[0:NM, P * b:P * b + P], ps[0:NM, 1, 0:P], ACT.Copy)\
                        .then_inc(dt_copied, 1)
                h, step = divmod(u - 5, 4)
                if step == 0 and 0 <= h < DH:
                    act.wait_ge(do_ready, h + 1)
                    nc.scalar.activation(qq[:, h, NM:T], ps[:, 2 + h % 2, :], ACT.Copy)
                    nc.scalar.activation(kk[:, h, NM:T], ps[:, 2 + h % 2, :], ACT.Square).then_inc(do_squared, 1)
                    if h == DH - 1:
                        act.dma_start(res[:], x_t).then_inc(res_in, 16)
                if step == 2 and 0 <= h < DH:
                    act.wait_ge(do_summed, h + 1)
                    root(kk[:, h, NM:T], ps[:, 2 + h % 2, :], 1.0 / (2 * DHD))
                if step == 0 and h > 0:
                    act.wait_ge(do_scaled, h)
                    hi_of(bh[:, h - 1, NM:T], qq[:, h - 1, NM:T])
            n_hi += DH
            gates_out(START["diff_out"], SEQ)
            for c in range(KC):
                act.wait_ge(mrg_ready, c + 1)
                if c == 0:
                    act.wait_ge(mm_done, START["diff_out"] + 16)
                hi_of(xh[:, c, NM:T], mrg[:, c, NM:T])
            n_hi += KC
            splits_and_root(START["w_out"], res, SEQ)

            norm_hi(SEQ)
            n_hf += KC
            for g in range(4):
                B = START[f"ffn{g}up"]
                with act.Fori(0, KC // 2) as i:
                    for j in range(2):
                        p0, p1 = pos(B, j, i), pos(B, j + 1, i)
                        begin(p0, p1)
                        nc.scalar.activation(tmp[:, j, NM:T], slot_ap(p0[2], SEQ), ACT.Relu).then_inc(relu_ready, 1)
                        act.wait_ge(evicted[p0[2]], p0[1] + 1)
                        hi_of(flat(bh[:, bass.ds(2 * i + j, 1), NM:T]), hf[:, j, NM:T])
                n_hi += KC
                if g < 3:
                    splits(START[f"ffn{g}down"], KC)
            splits_and_root(START["ffn3down"], res, SEQ)

            act.dma_start(res[:, :, 0:NM], meta2_t).then_inc(meta_in, 16)
            act.dma_start(glm[:], gla_masks).then_inc(const2_in, 16)
            act.dma_start(lrw[:], wgk).then_inc(const2_in, 16)
            act.wait_ge(meta_in, 16)
            norm(res, T, lambda c: act.wait_ge(h_ready, c + 1))
            act.dma_start(res_dram, res[:]).then_inc(res_saved, 16)
            norm_hi(T)
            n_hf += KC
            splits(START["sb_qkv"], 8)
            value_tiles(START["sb_qkv"] + 8, 4, 16)
            act.wait_ge(res_saved, 16)
            def softplus_part(h):
                k = h % 2
                for n, (dst, src) in enumerate(stick_pieces(h)):
                    act.wait_ge(sz_ready, 2 * h + 1 + min(n, 1))
                    nc.scalar.activation(dst, src, ACT.Abs).then_inc(sabs_done, 1)
                act.wait_ge(sabs_done, 4 * h + 4)
                link(nc.scalar.activation(sbt[k], sbt[k], ACT.Exp, scale=-1.0))
                link(nc.scalar.activation(sbm[k], sbm[k], ACT.Exp, scale=-1.0))
                nc.scalar.activation(sbt[k], sbt[k], ACT.Ln, bias=1.0).then_inc(slog_done, 1)
                nc.scalar.activation(sbm[k], sbm[k], ACT.Ln, bias=1.0).then_inc(slog_done, 1)

            def stick_weights(h):
                act.wait_ge(scum_done, h + 1)
                for dst, src in stick_pieces(h):
                    nc.scalar.activation(dst, src, ACT.Exp).then_inc(sw_done, 1)

            def stick_output(h):
                z = 4 * (h % 2)
                act.wait_ge(so_ready, h + 1)
                f = slice(SHD * (h % 2), SHD * (h % 2) + SHD)
                nc.scalar.activation(bh[f, h // 2, NM:T], ps[f, z, :], ACT.Copy)
                nc.scalar.activation(bh[f, h // 2, 0:NM], ps[f, z + 3, 0:NM], ACT.Copy).then_inc(so_hi, 1)

            softplus_part(0)
            softplus_part(1)
            for h in range(0, SH, 2):
                stick_weights(h)
                stick_weights(h + 1)
                for w in (h, h + 1):
                    stick_output(w)
                    if w + 2 < SH:
                        softplus_part(w + 2)
            gates_out(START["sb_out"], T)
            p_last = pos(START["sb_out"], 15)
            act.wait_ge(evicted[p_last[2]], p_last[1] + 1)
            act.dma_start(mrg_dram, mrg[:]).then_inc(mrg_saved, 16)

            splits_one(START["gla_lr"])
            for h in range(GH):
                act.wait_ge(gy_ready, h + 1)
                y = ps[:, 4 + 2 * (h % 2):6 + 2 * (h % 2), 0:HALF]
                if h >= 2:
                    act.wait_ge(glog_done, h - 1)
                link(nc.scalar.activation(two(grow[h % 2]), y, ACT.Abs, bias=wcol("b_gk_2", h)))
                act.wait_ge(gy_abs, h + 1)
                link(nc.scalar.activation(grow[h % 2], grow[h % 2], ACT.Exp, scale=-1.0))
                nc.scalar.activation(grow[h % 2], grow[h % 2], ACT.Ln, bias=1.0).then_inc(gy_log, 1)
            splits(START["gla_qkv"], 8)
            value_tiles(START["gla_qkv"] + 8, 8, 20)
            def prepare(h, part):
                cum, qc, kh, st = cums[h % 2], qcs[h], khs[h], 8 * (h % 2)
                if part == 0:
                    act.wait_ge(gcum_done, 2 * h + 1)
                    nc.scalar.activation(qc, cum, ACT.Exp, scale=1 / GATE_TAU)
                    nc.scalar.activation(stat[:, st:st + 1], cum[:, NM - 1:NM], ACT.Exp, scale=1 / GATE_TAU)
                    nc.scalar.activation(stat[:, st + 1:st + 5], cum[:, NM + P - 1:T:P], ACT.Exp, scale=1 / GATE_TAU)\
                        .then_inc(gexp_done, 1)
                    act.wait_ge(gcum_done, 2 * h + 2)
                    nc.scalar.activation(kh, kh, ACT.Exp, scale=1 / GATE_TAU).then_inc(gexp_done, 1)
                for k, L, lo in levels()[2 * part - 2:2 * part] if part else ():
                    m = 7 * h + k
                    act.wait_ge(gd_ready, m + 1)
                    nc.scalar.activation(grow[m % 2][:, lo:T], grow[m % 2][:, lo:T], ACT.Exp, scale=1 / GATE_TAU)\
                        .then_inc(ge_ready, 1)

            for part in range(5):
                prepare(0, part)
            for h in range(GH):
                for c in range(5):
                    if c < 4:
                        act.wait_ge(gt_ready, 4 * h + c + 1)
                        _, C = chunk(c)
                        nc.scalar.activation(ktok[c % 2][0:C, :], ps[0:C, 2, P:2 * P], ACT.Copy).then_inc(gt_copied, 1)
                    else:
                        act.wait_ge(go_ready, h + 1)
                        o = otile(h, 0)
                        nc.scalar.activation(kk[:, o:o + 2, NM:T], ps[:, 0:2, :], ACT.Copy)
                        nc.scalar.activation(kk[:, o:o + 2, 0:NM],
                                             ps[:, 2, 0:2 * NM].rearrange("p (v t) -> p v t", v=2),
                                             ACT.Copy).then_inc(go_copied, 1)
                    if h + 1 < GH:
                        prepare(h + 1, c)
            act.wait_ge(mrg_saved, 16)
            act.dma_start(mrg[:], mrg_dram).then_inc(mrg_back, 16)
            for h in range(GH):
                for v in range(2):
                    sum_squares(kk[:, otile(h, v), :], lambda: act.wait_ge(go_copied, GH))
                act.wait_ge(sq_used, n_sq)
                b = 4 + 2 * (h % 2)
                root(two(srow[h]), ps[:, b:b + 2, 0:HALF], 1.0 / GDV)
            B = START["gla_gate"]
            table_set(SILU)
            with act.Fori(0, KC // 2) as i:
                for j in range(2):
                    p0, p1 = pos(B, j, i), pos(B, j + 1, i)
                    begin(p0, p1)
                    act.wait_ge(hf_ready, n_hf + 2 * i + j)
                    nc.scalar.activation(two(gate[:, :]), slot_ap(p0[2], T), ACT.Silu).then_inc(evicted[p0[2]], 1)
                    act.wait_ge(hf_ready, n_hf + 2 * i + j + 1)
                    hi_of(flat(bh[:, bass.ds(2 * i + j, 1), :]), hf[:, j, :])
            n_hf += KC
            n_hi += KC
            act.dma_start(res[:], res_dram).then_inc(res_back, 16)
            gates_out(START["gla_out"], T)
            for c in range(KC):
                act.wait_ge(mrg_ready, KC + c + 1)
                if c == 0:
                    act.wait_ge(mm_done, START["gla_out"] + 16)
                hi_of(xh[:, c, :], mrg[:, c, :])
            n_hi += KC
            splits_and_root(START["w_o"], mrg, T)
            norm(res, T, lambda c: act.wait_ge(mix_added, c + 1))
            norm_hi(T)
            n_hf += KC
            tile = 0
            for g, n_g in enumerate(FFN2_GROUPS):
                B = START[f"glu{g}up"]
                table_set(GELU)
                with act.Fori(0, n_g // 2) as i:
                    for j in range(2):
                        up, gt, nx = pos(B, 2 * j, i, 4), pos(B, 2 * j + 1, i, 4), pos(B, 2 * j + 2, i, 4)
                        begin(up, gt)
                        nc.scalar.activation(two(tmp[:, j]), slot_ap(up[2], T), ACT.Copy).then_inc(evicted[up[2]], 1)
                        split_hi(*nx)
                        act.wait_ge(glu_copied, tile + 2 * i + j + 1)
                        nc.scalar.activation(gate[:, NM:T], hf[:, j, NM:T], ACT.Gelu_apprx_tanh).then_inc(glu_act, 1)
                        act.wait_ge(evicted[gt[2]], gt[1] + 1)
                        hi_of(flat(bh[:, bass.ds(2 * i + j, 1), NM:T]), hf[:, j, NM:T])
                tile += n_g
                n_hi += n_g
                if g == len(FFN2_GROUPS) - 1:
                    table_set(LN_EXP)
                    splits_and_root(START[f"glu{g}down"], mrg, SEQ)
                else:
                    splits(START[f"glu{g}down"], KC)
            for c in range(0, KC, 2):
                act.wait_ge(out_ready, c + 2)
                act.dma_start(out[:, c:c + 2], mrg[:, c:c + 2, NM:T]).then_inc(stored, 16)
            act.wait_ge(stored, 64)

        @block.vector
        def _(dve):
            link = Link(dve, dve_self)
            n_hi = n_root = n_x = n_b = n_added = 0
            n_sq = 0

            def split_lo(n, half, slot):
                dve.wait_ge(hi_done, n + 1)
                nc.vector.tensor_tensor(wl[:, slot], wraw[:, slot], wh[:, slot].bitcast(F32), ALU.subtract)\
                    .then_inc(lo_done, 1)

            def begin(this, next_one):
                split_lo(*next_one)
                dve.wait_ge(mm_done, this[0] + 1)

            def lo_of(dst, src, hi, ready, n):
                dve.wait_ge(hf_hi, n)
                nc.vector.tensor_tensor(dst, src, hi.bitcast(F32), ALU.subtract).then_inc(ready, 1)

            def root_made():
                nonlocal n_root
                n_root += 1
                dve.wait_ge(root_ready, n_root)

            def norm_apply(src, w, n):
                nonlocal n_hi, n_x
                root_made()
                tok = slice(T - n, T)
                for c in range(KC + 1):
                    if c < KC:
                        if c >= 2:
                            dve.wait_ge(x_ready, n_x + c - 1)
                        nc.vector.scalar_tensor_tensor(out=hf[:, c % 2, tok], in0=src[:, c, tok], scalar=wcol(w, c),
                                                       in1=rsq[:, tok], op0=ALU.mult, op1=ALU.mult)\
                            .then_inc(hf_ready, 1)
                    if c:
                        d = c - 1
                        dve.wait_ge(hf_ready, n_hf + c)
                        lo_of(xl[:, d, tok], hf[:, d % 2, tok], xh[:, d, tok], x_ready, n_hi + d + 1)
                n_hi += KC
                n_x += KC

            link(nc.vector.memset(small[:], EPS))
            nc.vector.nop().then_inc(eps_set, 1)
            dve.wait_ge(params_in, 48)
            for k in range(2):
                if k:
                    dve.wait_ge(lam_sums, 1)
                a, b = lamr[:, 128 * k:128 * k + 64], lamr[:, 128 * k + 64:128 * k + 128]
                nc.vector.tensor_tensor_reduce(out=a, in0=a, in1=b, scale=1.0, scalar=0.0, op0=ALU.mult, op1=ALU.add,
                                               accum_out=small[:, 1 + k:2 + k]).then_inc(lam_sums, 1)
            dve.wait_ge(lam_exps, 1)
            link(nc.vector.tensor_tensor(small[:, 5:6], small[:, 4:5], small[:, 3:4], ALU.subtract))
            link(nc.vector.tensor_scalar(small[:, 5:6], small[:, 5:6], -LAM_INIT, None, ALU.add))
            link(nc.vector.tensor_scalar(wcol("diff_subln_w"), wcol("diff_subln_w"), 1.0 - LAM_INIT, None, ALU.mult))
            n_hf = 0

            norm_apply(res, "norm1_w", T)
            n_hf += KC
            split_lo(0, 0, 0)

            B = START["conv_in"]
            o = COLS["conv_w"][0]
            with link.loop(KC // 2, 2 * 3) as i:
                for j in range(2):
                    p = [pos(B, 3 * j + k, i, 6) for k in range(4)]
                    split_lo(*p[1])
                    begin(p[1], p[2])
                    dve.wait_ge(evicted[p[0][2]], p[0][1] + 1)
                    nc.vector.tensor_tensor(two(tmp[:, j]), slot_ap(p[1][2], T), two(gate[:, :]), ALU.mult)\
                        .then_inc(evicted[p[1][2]], 1)
                    dve.wait_ge(evicted[p[1][2]], p[1][1] + 1)
                    taps = [col[:, bass.ds(3 * (2 * i + j) + (o + k), 1)] for k in range(3)]
                    y = hf[:, j, NM:T]
                    link(nc.vector.tensor_scalar(y, tmp[:, j, NM - 2:T - 2], taps[0], None, ALU.mult))
                    for k in (1, 2):
                        link(nc.vector.scalar_tensor_tensor(out=y, in0=tmp[:, j, NM - 2 + k:T - 2 + k],
                                                            scalar=taps[k], in1=y, op0=ALU.mult, op1=ALU.add))
                    begin(p[2], p[3])
                    nc.vector.tensor_tensor(y, slot_ap(p[2][2], SEQ), y, ALU.mult).then_inc(evicted[p[2][2]], 1)
                    lo_of(flat(bl[:, bass.ds(2 * i + j, 1), NM:T]), y, flat(bh[:, bass.ds(2 * i + j, 1), NM:T]),
                          b_ready, n_hi + 2 * i + j + 1)
            n_hi += KC

            def summed_strips(B, n, take):
                nonlocal n_sq, n_added
                tok = slice(T - n, T)

                def add(c):
                    dve.wait_ge(sq_ready, n_sq + c + 1)
                    if c > 1:
                        dve.wait_ge(sq_added, n_added + c - 1)
                    nc.vector.tensor_tensor(hf[:, 0, tok], hf[:, 0, tok], tmp[:, c % 2, tok], ALU.add)\
                        .then_inc(sq_added, 1)

                for c in range(KC):
                    p = pos(B, c)
                    begin(p, pos(B, c + 1))
                    take(c, slot_ap(p[2], n)).then_inc(evicted[p[2]], 1)
                    if c >= 2:
                        add(c - 1)
                n_sq += KC
                n_added += KC - 2

            def branch_out(B, n, first, last=False):
                with dve.Fori(0, KC) as i:
                    p0, p1, p2 = pos(B, 0, i), pos(B, 1, i), pos(B, 2, i)
                    split_lo(*p1)
                    begin(p1, p2)
                    dve.wait_ge(evicted[p0[2]], p0[1] + 1)
                    m = flat(mrg[:, bass.ds(i, 1), T - n:T])
                    m = m if n == SEQ else two(m)
                    dst = m if first else row(tmp[:, 0], n)
                    nc.vector.tensor_tensor(dst, slot_ap(p1[2], n), row(gate[:, :], n), ALU.mult)\
                        .then_inc(evicted[p1[2]], 1)
                    if not first:
                        dve.wait_ge(evicted[p1[2]], p1[1] + 1)
                        nc.vector.tensor_tensor(m, m, row(tmp[:, 0], n), ALU.add).then_inc(mrg_ready if last else mrg_sum, 1)

            def store(B, count, dst, scale=None, n=T):
                with dve.Fori(0, count // 2) as i:
                    for j in range(2):
                        p0 = pos(B, j, i)
                        begin(p0, pos(B, j + 1, i))
                        d = flat(dst[:, bass.ds(2 * i + j, 1), :])
                        if scale is None:
                            ins = nc.vector.tensor_copy(two(d), slot_ap(p0[2], T))
                        else:
                            ins = nc.vector.tensor_scalar(two(d), slot_ap(p0[2], T), scale, None, ALU.mult)
                        ins.then_inc(evicted[p0[2]], 1)

            def store_values(B, count, done):
                def pair(i):
                    for j in range(2):
                        p0 = pos(B, j, i)
                        begin(p0, pos(B, j + 1, i))
                        if not isinstance(i, int):
                            dve.wait_ge(vtr_done, 2 * i + (done + j - 1))
                        nc.vector.tensor_copy(two(tmp[:, j]), slot_ap(p0[2], T)).then_inc(evicted[p0[2]], 1)

                first_then_loop(dve, count // 2, pair)

            branch_out(START["conv_out"], SEQ, True)

            B = START["ret_qkv"]
            store(B, 4, qq[:, 0:4])
            store(B + 4, 4, qq[:, 4:8], P ** -0.5)
            store_values(B + 8, 8, 0)
            n_mask = 0
            for h in range(RH + 1):
                if h < RH:
                    dve.wait_ge(table_in[h % 2], 16 * (h // 2 + 1))
                    if h:
                        dve.wait_ge(ro_ready, h)
                    for t, q0 in key_tiles():
                        dve.wait_ge(rz_ready, 4 * h + min(t, 3) + 1)
                        if t == 0:
                            o_, s_, m_ = atm[0:NM, :], ps[0:NM, 4, :], tbl[h % 2][0:NM, NM:T]
                        else:
                            L = SEQ - q0
                            s_ = ps[:, 4 + t, 0:L] if t < 4 else ps[:, 7, 256:256 + L]
                            o_, m_ = at[:, t - 1, q0:SEQ], tbl[h % 2][:, 0:L]
                        nc.vector.tensor_tensor(o_, s_, m_, ALU.mult).then_inc(rs_masked, 1)
                if h:
                    w = h - 1
                    dve.wait_ge(mean_ready, w + 1)
                    for v in range(2):
                        y = kk[:, 2 * w + v, NM:T]
                        nc.vector.scalar_tensor_tensor(out=y, in0=ps[:, 2 * (w % 2), :], scalar=-1.0 / RDV, in1=y,
                                                       op0=ALU.mult, op1=ALU.add).then_inc(centred, 1)
                if h > 1 or h == RH:
                    for w in (h - 2, h - 1) if h == RH else (h - 2,):
                        root_made()
                        dve.wait_ge(centred, 2 * w + 2)
                        for v in range(2):
                            y = kk[:, 2 * w + v, NM:T]
                            nc.vector.tensor_tensor(y, y, qq[:, w, NM:T], ALU.mult).then_inc(r_scaled, 1)
            dve.wait_ge(r_scaled, 2 * RH)
            B = START["ret_gate"]
            with dve.Fori(0, KC // 2) as i:
                for j in range(2):
                    p0 = pos(B, j, i)
                    begin(p0, pos(B, j + 1, i))
                    dve.wait_ge(evicted[p0[2]], p0[1] + 1)
                    c = bass.ds(2 * i + j, 1)
                    nc.vector.tensor_tensor(hf[:, j, NM:T], gate[:, NM:T], flat(kk[:, c, NM:T]), ALU.mult)\
                        .then_inc(hf_ready, 1)
                    dve.wait_ge(hf_ready, n_hf + 2 * i + j + 1)
                    lo_of(flat(bl[:, c, NM:T]), hf[:, j, NM:T], flat(bh[:, c, NM:T]), b_ready, n_hi + 2 * i + j + 1)
            n_hf += KC
            n_hi += KC
            branch_out(START["ret_out"], SEQ, False)

            B = START["diff_qkv"]
            store(B, 8, qq)
            store(B + 8, 8, kk)
            store_values(B + 16, 8, 8)
            for u in range(4 * DH + 7):
                if u < 4 * DH:
                    h, b = divmod(u, 4)
                    L, j0 = NM + P * (b + 1), P * (3 - b)
                    if b == 0:
                        dve.wait_ge(table_in[h % 2], 32 + 16 * (h // 2 + 1))
                    if u >= 2:
                        dve.wait_ge(da_ready, u - 1)
                    for m in range(2):
                        c = 2 * (u % 2) + m
                        dve.wait_ge(dz_ready, 2 * u + m + 1)
                        src = ps[:, 4 + 2 * m:6 + 2 * m, :].rearrange("p b q -> p (b q)")[:, 0:L]
                        nc.vector.tensor_tensor_reduce(
                            out=prob[u % 2][m][:, 0:L], in0=src, in1=tbl[h % 2][:, j0:T], scale=1.0, scalar=-3e38,
                            op0=ALU.add, op1=ALU.max, accum_out=stat[:, c:c + 1]).then_inc(ds_ready, 1)
                    dve.wait_ge(ds_ready, 2 * u + 2)
                    c = 2 * (u % 2)
                    nc.vector.tensor_scalar(stat[:, 4 + c:6 + c], stat[:, c:c + 2], -DHD ** -0.5, None,
                                            ALU.mult).then_inc(dmax_ready, 1)
                if 0 < u <= 4 * DH:
                    w = u - 1
                    h, b = divmod(w, 4)
                    L = NM + P * (b + 1)
                    p1, p2 = (prob[w % 2][m][:, 0:L] for m in range(2))
                    c = 8 + 2 * (w % 2)
                    dve.wait_ge(dp_ready, 2 * w + 2)
                    link(nc.vector.reciprocal(stat[:, c + 4:c + 6], stat[:, c:c + 2]))
                    link(nc.vector.tensor_tensor(stat[:, c + 5:c + 6], stat[:, c + 5:c + 6], small[:, 5:6], ALU.mult))
                    link(nc.vector.tensor_scalar(p2, p2, stat[:, c + 5:c + 6], None, ALU.mult))
                    if w >= 2:
                        dve.wait_ge(dt_ready, w - 1)
                    nc.vector.scalar_tensor_tensor(out=tmp[:, w % 2, 0:L], in0=p1, scalar=stat[:, c + 4:c + 5],
                                                   in1=p2, op0=ALU.mult, op1=ALU.add).then_inc(da_ready, 1)
                h, step = divmod(u - 8, 4)
                if step == 0 and 0 <= h < DH:
                    root_made()
                    nc.vector.scalar_tensor_tensor(out=qq[:, h, NM:T], in0=qq[:, h, NM:T],
                                                   scalar=wcol("diff_subln_w"), in1=kk[:, h, NM:T],
                                                   op0=ALU.mult, op1=ALU.mult).then_inc(do_scaled, 1)
                if step == 2 and 0 <= h < DH:
                    dve.wait_ge(do_scaled, h + 1)
                    lo_of(bl[:, h, NM:T], qq[:, h, NM:T], bh[:, h, NM:T], b_ready, n_hi + h + 1)
            n_hi += DH
            branch_out(START["diff_out"], SEQ, False, True)
            for c in range(KC):
                lo_of(xl[:, c, NM:T], mrg[:, c, NM:T], xh[:, c, NM:T], x_ready, n_hi + c + 1)
            n_hi += KC
            n_x += KC

            def accumulate(B, n=SEQ):
                with dve.Fori(0, KC // 2) as i:
                    for j in range(2):
                        p0 = pos(B, j, i)
                        begin(p0, pos(B, j + 1, i))
                        r = flat(res[:, bass.ds(2 * i + j, 1), T - n:T])
                        nc.vector.tensor_tensor(r, slot_ap(p0[2], n), r, ALU.add).then_inc(evicted[p0[2]], 1)

            dve.wait_ge(res_in, 16)

            def add_to_res(c, src):
                return nc.vector.tensor_tensor(res[:, c, NM:T], src, res[:, c, NM:T], ALU.add)

            n_sq += KC + 2 * RH
            summed_strips(START["w_out"], SEQ, add_to_res)
            norm_apply(res, "norm2_w", SEQ)
            n_hf += KC
            for g in range(4):
                B = START[f"ffn{g}up"]
                with dve.Fori(0, KC // 2) as i:
                    for j in range(2):
                        p0 = pos(B, j, i)
                        begin(p0, pos(B, j + 1, i))
                        dve.wait_ge(relu_ready, KC * g + 2 * i + j + 1)
                        dve.wait_ge(b_ready, (3 + g) * KC + 2 * i + j - 1)
                        nc.vector.scalar_tensor_tensor(out=hf[:, j, NM:T], in0=slot_ap(p0[2], SEQ), scalar=0.0,
                                                       in1=tmp[:, j, NM:T], op0=ALU.max, op1=ALU.mult)\
                            .then_inc(evicted[p0[2]], 1)
                        c = bass.ds(2 * i + j, 1)
                        lo_of(flat(bl[:, c, NM:T]), hf[:, j, NM:T], flat(bh[:, c, NM:T]), b_ready,
                              n_hi + 2 * i + j + 1)
                n_hi += KC
                if g < 3:
                    accumulate(START[f"ffn{g}down"])
            summed_strips(START["ffn3down"], SEQ, add_to_res)
            root_made()
            for c in range(KC):
                y = res[:, c, NM:T]
                nc.vector.scalar_tensor_tensor(out=y, in0=y, scalar=wcol("final_norm_w", c), in1=rsq[:, NM:T],
                                               op0=ALU.mult, op1=ALU.mult).then_inc(h_ready, 1)

            norm_apply(res, "norm_mix_pre_2", T)
            n_hf += KC
            B = START["sb_qkv"]
            store(B, 4, qq[:, 0:4], SHD ** -0.5)
            store(B + 4, 4, qq[:, 4:8])
            store_values(B + 8, 4, 16)
            def softplus(h):
                for n, (dst, src) in enumerate(stick_pieces(h)):
                    dve.wait_ge(slog_done, 2 * h + 1 + (n > 1))
                    nc.vector.scalar_tensor_tensor(out=dst, in0=src, scalar=0.0, in1=dst, op0=ALU.max,
                                                   op1=ALU.add).then_inc(sp_done, 1)

            def stick_output(h):
                z, f = 4 * (h % 2), slice(SHD * (h % 2), SHD * (h % 2) + SHD)
                dve.wait_ge(so_hi, h + 1)
                nc.vector.tensor_tensor(bl[f, h // 2, NM:T], ps[f, z, :], bh[f, h // 2, NM:T].bitcast(F32),
                                        ALU.subtract)
                nc.vector.tensor_tensor(bl[f, h // 2, 0:NM], ps[f, z + 3, 0:NM], bh[f, h // 2, 0:NM].bitcast(F32),
                                        ALU.subtract).then_inc(b_ready, 1)

            softplus(0)
            softplus(1)
            for h in range(SH):
                stick_output(h)
                if h + 2 < SH:
                    softplus(h + 2)
            branch_out(START["sb_out"], T, True)

            p0 = pos(START["gla_lr"])
            begin(p0, pos(START["gla_lr"], 1))
            nc.vector.tensor_copy(two(tmp[0:NM, 0]), ps[0:NM, 2 * p0[2]:2 * p0[2] + 2, 0:HALF])\
                .then_inc(evicted[p0[2]], 1)
            dve.wait_ge(const2_in, 32)
            for h in range(GH):
                dve.wait_ge(gy_ready, h + 1)
                y = ps[:, 4 + 2 * (h % 2):6 + 2 * (h % 2), 0:HALF]
                dve.wait_ge(act_self, 2 * SH + 2 * h + 1)
                nc.vector.tensor_scalar(two(kk[:, h, :]), y, wcol("b_gk_2", h), 0.0, ALU.add, ALU.min)\
                    .then_inc(gy_abs, 1)
                dve.wait_ge(gy_log, h + 1)
                dve.wait_ge(gy_abs, h + 1)
                nc.vector.tensor_tensor(kk[:, h, :], kk[:, h, :], grow[h % 2], ALU.subtract).then_inc(glog_done, 1)
            B = START["gla_qkv"]
            store(B, 4, qq[:, 0:4], P ** -0.5)
            store(B + 4, 4, qq[:, 4:8])
            store_values(B + 8, 8, 20)
            link(nc.vector.memset(gtmp, 1.0))
            link(nc.vector.memset(gtmp[:, 0:1], 0.0))
            link(nc.vector.memset(gtmp[:, NM:T:P], 0.0))
            def factors(h, k, L, lo):
                m = 7 * h + k
                x, e = halves(xl_rows[h % 2][k], L, lo), halves(grow[m % 2], L, lo)
                dve.wait_ge(ge_ready, m + 1)
                nc.vector.tensor_tensor(x[:, :, 0, :], halves(qq[:, 4 + h, :], L, lo)[:, :, 0, :], e[:, :, 0, :],
                                        ALU.mult)
                nc.vector.tensor_tensor(x[:, :, 1, :], halves(qq[:, h, :], L, lo)[:, :, 1, :], e[:, :, 1, :],
                                        ALU.mult).then_inc(gx_ready, 1)

            def prepare(h, part):
                cum, qc, kh = cums[h % 2], qcs[h], khs[h]
                if part == 0:
                    if h >= 2:
                        dve.wait_ge(go_ready, h - 1)
                    nc.vector.tensor_tensor_scan(cum, gtmp, kk[:, h, :], 0.0, ALU.mult, ALU.add).then_inc(gcum_done, 1)
                    dve.wait_ge(gcum_done, 2 * h + 1)
                    link(nc.vector.tensor_tensor(kh[:, 0:NM], cum[:, NM - 1:NM].to_broadcast([P, NM]), cum[:, 0:NM],
                                                 ALU.subtract))
                    c3, k3 = (r[:, NM:T].rearrange("p (c t) -> p c t", c=4) for r in (cum, kh))
                    nc.vector.tensor_tensor(k3, c3[:, :, P - 1:P].to_broadcast([P, 4, P]), c3, ALU.subtract)\
                        .then_inc(gcum_done, 1)
                if part == 1:
                    dve.wait_ge(gexp_done, 2 * h + 2)
                    link(nc.vector.tensor_tensor(qc, qc, qq[:, h, :], ALU.mult))
                    link(nc.vector.tensor_tensor(kh, kh, qq[:, 4 + h, :], ALU.mult))
                    factors(h, *levels()[0])
                if part > 1:
                    factors(h, *levels()[2 * part - 3])
                    factors(h, *levels()[2 * part - 2])

            for part in range(5):
                prepare(0, part)
            dve.wait_ge(mrg_saved, 16)
            for h in range(GH):
                for c in range(5):
                    u = 5 * h + c
                    _, C = chunk(c)
                    l0 = 3 if c == 0 else 0
                    dve.wait_ge(gp_ready, u + 1)
                    if u:
                        dve.wait_ge(ga_ready, u)
                    b = 4 + 2 * (c % 2)
                    src = ps[0:C, b:b + 2, :].rearrange("p b (l t) -> p (b l) t", t=P)[:, l0:8, 0:C]
                    nc.vector.tensor_tensor(masked[0:C, l0:8, 0:C], src, glm[0:C, l0:8, 0:C], ALU.mult)\
                        .then_inc(gp_used, 1)
                    dve.wait_ge(gp_used, u + 1)
                    if c >= 2:
                        dve.wait_ge(gs_ready, 4 * h + c - 1)
                    elif c == 0 and h:
                        dve.wait_ge(go_ready, h)
                    nc.vector.tensor_reduce(amat[c % 2][0:C, 0:C],
                                            masked[0:C, l0:8, 0:C].rearrange("p l t -> p t l"), AX, ALU.add)\
                        .then_inc(ga_ready, 1)
                    if h + 1 < GH:
                        prepare(h + 1, c)
                    if c < 4:
                        dve.wait_ge(gs_ready, 4 * h + c + 1)
                    if c == 0:
                        nc.vector.tensor_copy(state[0], ps[:, 3, 0:GDV]).then_inc(gs_done, 1)
                    elif c < 4:
                        dve.wait_ge(gs_done, 4 * h + c)
                        k = 8 * (h % 2) + c
                        nc.vector.scalar_tensor_tensor(out=state[c % 2], in0=state[(c - 1) % 2],
                                                       scalar=stat[:, k:k + 1], in1=ps[:, 3, 0:GDV], op0=ALU.mult,
                                                       op1=ALU.add).then_inc(gs_done, 1)
            for h in range(GH):
                root_made()
                for v in range(2):
                    o = kk[:, otile(h, v), :]
                    link(nc.vector.scalar_tensor_tensor(out=o, in0=o, scalar=wcol("gla_head_norm_2", v),
                                                        in1=srow[h], op0=ALU.mult, op1=ALU.mult))
            B = START["gla_gate"]
            with dve.Fori(0, KC // 2) as i:
                for j in range(2):
                    p0 = pos(B, j, i)
                    begin(p0, pos(B, j + 1, i))
                    dve.wait_ge(evicted[p0[2]], p0[1] + 1)
                    c = bass.ds(2 * i + j, 1)
                    nc.vector.tensor_tensor(hf[:, j, :], gate[:, :], flat(kk[:, c, :]),
                                            ALU.mult).then_inc(hf_ready, 1)
                    dve.wait_ge(hf_ready, n_hf + 2 * i + j + 1)
                    lo_of(flat(bl[:, c, :]), hf[:, j, :], flat(bh[:, c, :]), b_ready, n_hi + 2 * i + j + 1)
            n_hf += KC
            n_hi += KC
            dve.wait_ge(mrg_back, 16)
            branch_out(START["gla_out"], T, False, True)
            for c in range(KC):
                lo_of(xl[:, c, :], mrg[:, c, :], xh[:, c, :], x_ready, n_hi + c + 1)
            n_hi += KC
            n_x += KC
            dve.wait_ge(x_ready, n_x)
            n_sq += KC + 2 * GH
            summed_strips(START["w_o"], T, lambda c, src: nc.vector.tensor_copy(two(mrg[:, c, :]), src))
            root_made()
            dve.wait_ge(res_back, 16)
            for c in range(KC):
                link(nc.vector.scalar_tensor_tensor(out=mrg[:, c, :], in0=mrg[:, c, :],
                                                    scalar=wcol("norm_mix_post_2", c), in1=rsq[:, :],
                                                    op0=ALU.mult, op1=ALU.mult))
                nc.vector.tensor_tensor(res[:, c, :], res[:, c, :], mrg[:, c, :], ALU.add).then_inc(mix_added, 1)
            norm_apply(res, "norm_ffn_pre_2", T)
            n_hf += KC
            tile = 0
            for g, n_g in enumerate(FFN2_GROUPS):
                B = START[f"glu{g}up"]
                oc, ob = COLS["conv_w_2"][0] + 3 * tile, COLS["conv_b_2"][0] + tile
                with link.loop(n_g // 2, 4) as i:
                    for j in range(2):
                        up, gt, nx = pos(B, 2 * j, i, 4), pos(B, 2 * j + 1, i, 4), pos(B, 2 * j + 2, i, 4)
                        split_lo(*gt)
                        dve.wait_ge(evicted[up[2]], up[1] + 1)
                        taps = [col[:, bass.ds(3 * (2 * i + j) + (oc + k), 1)] for k in range(3)]
                        y = hf[:, j, NM:T]
                        dve.wait_ge(b_ready, 8 * KC + SH + tile + 2 * i + j - 1)
                        link(nc.vector.tensor_scalar(y, tmp[:, j, NM - 2:T - 2], taps[0],
                                                     col[:, bass.ds(2 * i + (ob + j), 1)], ALU.mult, ALU.add))
                        for k in (1, 2):
                            ins = nc.vector.scalar_tensor_tensor(out=y, in0=tmp[:, j, NM - 2 + k:T - 2 + k],
                                                                 scalar=taps[k], in1=y, op0=ALU.mult, op1=ALU.add)
                            if k == 1:
                                link(ins)
                            else:
                                ins.then_inc(glu_copied, 1)
                        begin(gt, nx)
                        dve.wait_ge(glu_act, tile + 2 * i + j + 1)
                        nc.vector.tensor_tensor(y, slot_ap(gt[2], SEQ), gate[:, NM:T], ALU.mult)\
                            .then_inc(evicted[gt[2]], 1)
                        c = bass.ds(2 * i + j, 1)
                        lo_of(flat(bl[:, c, NM:T]), y, flat(bh[:, c, NM:T]), b_ready, n_hi + 2 * i + j + 1)
                tile += n_g
                n_hi += n_g
                if g == len(FFN2_GROUPS) - 1:
                    break
                B = START[f"glu{g}down"]
                with dve.Fori(0, KC // 2) as i:
                    for j in range(2):
                        p0 = pos(B, j, i)
                        begin(p0, pos(B, j + 1, i))
                        m = flat(mrg[:, bass.ds(2 * i + j, 1), NM:T])
                        if g == 0:
                            ins = nc.vector.tensor_copy(m, slot_ap(p0[2], SEQ))
                        else:
                            ins = nc.vector.tensor_tensor(m, slot_ap(p0[2], SEQ), m, ALU.add)
                        ins.then_inc(evicted[p0[2]], 1)
            n_sq += KC
            summed_strips(START[f"glu{g}down"], SEQ, lambda c, src: nc.vector.tensor_tensor(
                mrg[:, c, NM:T], src, mrg[:, c, NM:T], ALU.add))
            root_made()
            for c in range(KC):
                m = mrg[:, c, NM:T]
                link(nc.vector.scalar_tensor_tensor(out=m, in0=m, scalar=wcol("norm_ffn_post_2", c),
                                                    in1=rsq[:, NM:T], op0=ALU.mult, op1=ALU.mult))
                nc.vector.tensor_tensor(m, m, res[:, c, NM:T], ALU.add).then_inc(out_ready, 1)

        @block.tensor
        def _(pe):
            n_sq = n_added = 0

            def strip(p, src, n, chunks=range(KC), dst=None, ready=None, wchunk=lambda c: c):
                number, half, slot = p
                hi, lo = (xh, xl) if src == "x" else (bh, bl)
                pe.wait_ge(lo_done, number + 1)
                if not (isinstance(half, int) and half == 0):
                    pe.wait_ge(evicted[slot], half)
                rows = [(slice(NM, T), ps[:, 2 * slot, :])] if n == SEQ else \
                    [(slice(HALF * k, HALF * k + HALF), ps[:, 2 * slot + k, 0:HALF]) for k in range(2)]
                for c in chunks:
                    if ready is not None:
                        pe.wait_ge(ready[0], ready[1] + c + 1)
                    for w, a in ((wh, hi), (wh, lo), (wl, hi)):
                        for tok, o in rows:
                            last = nc.tensor.matmul(o, w[:, slot, wchunk(c), :], a[:, c, tok],
                                                    start=(c == chunks[0] and w is wh and a is hi),
                                                    stop=(c == chunks[-1] and w is wl))
                last.then_inc(mm_done, 1)

            def strips(B, count, src, n, ready=None, chunks=range(KC)):
                lo = 0
                if ready is not None:
                    for j in range(2):
                        strip(pos(B, j), src, n, chunks=chunks, ready=ready if j == 0 else None)
                    lo = 1
                with pe.Fori(lo, count // 2) as i:
                    for j in range(2):
                        strip(pos(B, j, i), src, n, chunks=chunks)

            def sum_rows(bank, rows, n=SEQ, squares=True):
                nonlocal n_sq
                for k in range(rows):
                    pe.wait_ge(sq_ready, n_sq + 1)
                    for tok, o in ([(slice(NM, T), ps[:, bank, :])] if n == SEQ else
                                   [(slice(HALF * q, HALF * q + HALF), ps[:, bank + q, 0:HALF]) for q in range(2)]):
                        last = nc.tensor.matmul(o, ones, tmp[:, n_sq % 2, tok], start=(k == 0), stop=(k == rows - 1))
                    last.then_inc(sq_used, 1)
                    n_sq += 1

            def strips_and_sums(B, src, n, ready, chunks=range(KC)):
                nonlocal n_sq, n_added
                strips(B, KC, src, n, ready, chunks)
                n_sq += KC
                n_added += KC - 2
                pe.wait_ge(sq_added, n_added)
                pe.wait_ge(sq_ready, n_sq)
                for k, squares in enumerate((hf[:, 0, :], tmp[:, 1, :])):
                    for tok, o in ([(slice(NM, T), ps[:, 4, :])] if n == SEQ else
                                   [(slice(HALF * q, HALF * q + HALF), ps[:, 4 + q, 0:HALF]) for q in range(2)]):
                        last = nc.tensor.matmul(o, ones, squares[:, tok], start=(k == 0), stop=(k == 1))
                last.then_inc(sq_used, KC)

            def value_strips(B, count, done):
                def turn(j, n, p):
                    pe.wait_ge(evicted[p[2]], p[1] + 1)
                    if not isinstance(n, int) or done + n > 0:
                        pe.wait_ge(vt_done, n + done)
                    for kb in range(4):
                        nc.tensor.transpose(ps[:, 6, P * kb:P * kb + P], tmp[:, j, NM + P * kb:NM + P * kb + P], ident)
                    nc.tensor.transpose(ps[0:NM, 7, 0:P], tmp[:, j, 0:NM], ident).then_inc(vtr_done, 1)

                strip(pos(B, 0), "x", T)
                strip(pos(B, 1), "x", T)
                turn(0, 0, pos(B, 0))
                with pe.Fori(1, count // 2) as i:
                    for j in range(2):
                        strip(pos(B, j, i), "x", T)
                        turn(1 - j, 2 * i + (j - 1), pos(B, j - 1, i))
                turn(1, count - 1, pos(B, count - 1))

            pe.wait_ge(params_in, 48)
            sum_rows(4, KC, T)
            B = START["conv_in"]
            for k in range(6):
                strip(pos(B, k), "x", SEQ if k % 3 == 2 else T, ready=(x_ready, 0) if k == 0 else None)
            with pe.Fori(1, KC // 2) as i:
                for k in range(6):
                    strip(pos(B, k, i, 6), "x", SEQ if k % 3 == 2 else T)
            n_x = KC

            def branch_strips(B, n, readyb):
                strip(pos(B, 0), "x", n)
                strip(pos(B, 1), "b", n, ready=(b_ready, readyb))
                with pe.Fori(1, KC) as i:
                    strip(pos(B, 0, i), "x", n)
                    strip(pos(B, 1, i), "b", n)

            branch_strips(START["conv_out"], SEQ, 0)
            strips(START["ret_qkv"], 8, "x", T)
            value_strips(START["ret_qkv"] + 8, 8, 0)
            def scores(h):
                for t, q0 in key_tiles():
                    if h and t < 4:
                        pe.wait_ge(rs_masked, 5 * (h - 1) + (t + 1 if t < 3 else 5))
                    keys = qq[:, 4 + h, 0:NM] if t == 0 else qq[:, 4 + h, NM + q0:NM + q0 + P]
                    L = SEQ - q0
                    o = ps[0:NM, 4, :] if t == 0 else ps[:, 4 + t, 0:L] if t < 4 else ps[:, 7, 256:256 + L]
                    ins = nc.tensor.matmul(o, keys, qq[:, h, NM + q0:T], start=True, stop=True)
                    if t != 3:
                        ins.then_inc(rz_ready, 1)

            def products(h):
                pe.wait_ge(rs_masked, 5 * h + 5)
                if h >= 2:
                    pe.wait_ge(root_ready, 1 + h - 1)
                for v in range(2):
                    f = RDV * h + P * v
                    for t, q0 in key_tiles():
                        o = ps[:, 2 * (h % 2) + v, q0:SEQ]
                        if t == 0:
                            nc.tensor.matmul(o, vt[0:NM, 0, f:f + P], atm[0:NM, :], start=True, stop=False)
                        else:
                            ins = nc.tensor.matmul(o, vt[:, t, f:f + P], at[:, t - 1, q0:SEQ], start=False,
                                                   stop=(t == 4))
                ins.then_inc(ro_ready, 1)

            def mean(h):
                pe.wait_ge(ro_copied, h + 1)
                for v in range(2):
                    ins = nc.tensor.matmul(ps[:, 2 * (h % 2), :], ones, kk[:, 2 * h + v, NM:T], start=(v == 0),
                                           stop=(v == 1))
                ins.then_inc(mean_ready, 1)

            pe.wait_ge(vt_done, 8)
            scores(0)
            for h in range(RH):
                if h + 1 < RH:
                    scores(h + 1)
                if h:
                    mean(h - 1)
                products(h)
                if h:
                    sum_rows(2 * ((h - 1) % 2) + 1, 2)
            mean(RH - 1)
            strip(pos(START["ret_gate"], 0), "x", SEQ)
            sum_rows(2 * ((RH - 1) % 2) + 1, 2)
            strip(pos(START["ret_gate"], 1), "x", SEQ)
            with pe.Fori(1, KC // 2) as i:
                for j in range(2):
                    strip(pos(START["ret_gate"], j, i), "x", SEQ)
            branch_strips(START["ret_out"], SEQ, KC)
            strips(START["diff_qkv"], 16, "x", T)
            value_strips(START["diff_qkv"] + 16, 8, 8)
            pe.wait_ge(vt_done, 16)
            for u in range(4 * DH + 3):
                if u < 4 * DH:
                    h, b = divmod(u, 4)
                    L = NM + P * (b + 1)
                    for m in range(2):
                        if u:
                            pe.wait_ge(ds_ready, 2 * u - 1 + m)
                        f = slice(DHD * m, DHD * m + DHD)
                        q = qq[f, h, NM + P * b:NM + P * b + P]
                        for lo, hi in ((0, min(L, SEQ)), (SEQ, L)):
                            if lo < hi:
                                ins = nc.tensor.matmul(ps[:, 4 + 2 * m + lo // SEQ, 0:hi - lo], q, kk[f, h, lo:hi],
                                                       start=True, stop=True)
                        ins.then_inc(dz_ready, 1)
                if 2 <= u < 4 * DH + 2:
                    w = u - 2
                    h, b = divmod(w, 4)
                    pe.wait_ge(da_ready, w + 1)
                    if w:
                        pe.wait_ge(dt_copied, w)
                    a = tmp[:, w % 2]
                    for kb in range(b + 1):
                        nc.tensor.transpose(ps[:, 0, P * kb:P * kb + P], a[:, NM + P * kb:NM + P * kb + P], ident)
                    nc.tensor.transpose(ps[0:NM, 1, 0:P], a[:, 0:NM], ident).then_inc(dt_ready, 1)
                    if b == 3:
                        pe.wait_ge(dt_copied, w + 1)
                        if h >= 2:
                            pe.wait_ge(root_ready, 1 + RH + h - 1)
                        for t, q0 in key_tiles():
                            o = ps[:, 2 + h % 2, q0:SEQ]
                            if t == 0:
                                nc.tensor.matmul(o, vt[0:NM, 0, P * h:P * h + P], atm[0:NM, :], start=True,
                                                 stop=False)
                            else:
                                ins = nc.tensor.matmul(o, vt[:, t, P * h:P * h + P], at[:, t - 1, q0:SEQ],
                                                       start=False, stop=(t == 4))
                        ins.then_inc(do_ready, 1)
                h, step = divmod(u - 6, 4)
                if step == 0 and h >= 0:
                    pe.wait_ge(do_squared, h + 1)
                    nc.tensor.matmul(ps[:, 2 + h % 2, :], ones, kk[:, h, NM:T], start=True, stop=True)\
                        .then_inc(do_summed, 1)
            pe.wait_ge(dt_copied, 4 * DH)
            pe.wait_ge(root_ready, 1 + RH + DH - 1)
            branch_strips(START["diff_out"], SEQ, 2 * KC)
            strips_and_sums(START["w_out"], "x", SEQ, (x_ready, KC))
            for g in range(4):
                strips(START[f"ffn{g}up"], KC, "x", SEQ, ready=(x_ready, 2 * KC) if g == 0 else None)
                (strips_and_sums(START["ffn3down"], "b", SEQ, (b_ready, 6 * KC)) if g == 3 else
                 strips(START[f"ffn{g}down"], KC, "b", SEQ, ready=(b_ready, (3 + g) * KC)))

            sum_rows(4, KC, T)
            strips(START["sb_qkv"], 8, "x", T, ready=(x_ready, 3 * KC))
            value_strips(START["sb_qkv"] + 8, 4, 16)
            def logits(h):
                z, f = 4 * (h % 2), slice(SHD * (h % 2), SHD * (h % 2) + SHD)
                q, k = qq[f, h // 2], qq[f, 4 + h // 2]
                for t in range(4):
                    if t == 2 and h >= 2:
                        pe.wait_ge(b_ready, 7 * KC + h - 1)
                    o, L = sb_bank(z, t)
                    nc.tensor.matmul(o, k[:, NM + P * t:NM + P * t + P], q[:, NM + P * t:T], start=(t < 3),
                                     stop=True, skip_group_check=True)
                    ins = nc.tensor.matmul(o[:, 0:P], identb[:], negm[:], start=False, stop=True,
                                           skip_group_check=True)
                    if t == 0:
                        ins.then_inc(sz_ready, 1)
                nc.tensor.matmul(ps[0:NM, z, :], k[:, 0:NM], q[:, NM:T], start=True, stop=True)
                o = ps[0:NM, z + 3, 384:384 + NM]
                nc.tensor.matmul(o, k[:, 0:NM], q[:, 0:NM], start=False, stop=True, skip_group_check=True)
                nc.tensor.matmul(o, identb[0:NM, 0:NM], negm[0:NM, 0:NM], start=False, stop=True,
                                 skip_group_check=True).then_inc(sz_ready, 1)

            def sb_bank(z, t):
                L = SEQ - P * t
                return (ps[:, z + 1 + t, 0:L], L) if t < 3 else (ps[:, z + 3, 256:256 + L], L)

            def subtract_sums(h):
                k, z = h % 2, 4 * (h % 2)
                pe.wait_ge(sp_done, 4 * h + 4)
                for t in range(4):
                    o, L = sb_bank(z, t)
                    for t2 in range(t, 4):
                        L2 = SEQ - P * t2
                        nc.tensor.matmul(o[:, L - L2:L], ntri if t2 == t else nones, sbt[k][:, SB0[t2]:SB0[t2] + L2],
                                         start=False, stop=(t2 == 3), skip_group_check=True)
                o = ps[0:NM, z, :]
                for t2 in range(4):
                    L2 = SEQ - P * t2
                    nc.tensor.matmul(o[:, SEQ - L2:SEQ], nones[:, 0:NM], sbt[k][:, SB0[t2]:SB0[t2] + L2],
                                     start=False, stop=False, skip_group_check=True)
                nc.tensor.matmul(o, ntri[0:NM, 0:NM], sbm[k][:, NM:T], start=False, stop=True,
                                 skip_group_check=True)
                nc.tensor.matmul(ps[0:NM, z + 3, 384:384 + NM], ntri[0:NM, 0:NM], sbm[k][:, 0:NM], start=False,
                                 stop=True, skip_group_check=True).then_inc(scum_done, 1)

            def sb_products(h):
                k, z, f = h % 2, 4 * (h % 2), slice(SHD * (h % 2), SHD * (h % 2) + SHD)
                v = slice(SHD * h, SHD * h + SHD)
                pe.wait_ge(sw_done, 4 * h + 4)
                nc.tensor.matmul(ps[f, z, :], vt[0:NM, 0, v], sbm[k][:, NM:T], start=True, stop=False)
                for t in range(4):
                    L = SEQ - P * t
                    nc.tensor.matmul(ps[f, z, P * t:SEQ], vt[:, 1 + t, v], sbt[k][:, SB0[t]:SB0[t] + L],
                                     start=False, stop=(t == 3))
                nc.tensor.matmul(ps[f, z + 3, 0:NM], vt[0:NM, 0, v], sbm[k][:, 0:NM], start=True, stop=True)\
                    .then_inc(so_ready, 1)

            pe.wait_ge(vt_done, 20)
            pe.wait_ge(masks_made, 1)
            logits(0)
            logits(1)
            for h in range(0, SH, 2):
                subtract_sums(h)
                subtract_sums(h + 1)
                for w in (h, h + 1):
                    sb_products(w)
                    if w + 2 < SH:
                        logits(w + 2)
            pe.wait_ge(b_ready, 7 * KC + SH)
            with pe.Fori(0, KC) as i:
                strip(pos(START["sb_out"], 0, i), "x", T)
                strip(pos(START["sb_out"], 1, i), "b", T, chunks=range(4))
            p0 = pos(START["gla_lr"])
            strip(p0, "x", T)
            pe.wait_ge(evicted[p0[2]], p0[1] + 1)
            pe.wait_ge(const2_in, 32)
            for h in range(GH):
                if h >= 2:
                    pe.wait_ge(gy_abs, h - 1)
                for k in range(2):
                    ins = nc.tensor.matmul(ps[:, 4 + 2 * (h % 2) + k, 0:HALF], lrw[:, P * h:P * h + P],
                                           tmp[0:NM, 0, HALF * k:HALF * k + HALF], start=True, stop=True)
                ins.then_inc(gy_ready, 1)
            strips(START["gla_qkv"], 8, "x", T)
            value_strips(START["gla_qkv"] + 8, 8, 20)
            pe.wait_ge(vt_done, 28)

            def level_products(h, c):
                tok, C = chunk(c)
                u = 5 * h + c
                if c == 0:
                    pe.wait_ge(gx_ready, 7 * h + 7)
                if u >= 2:
                    pe.wait_ge(gp_used, u - 1)
                for k, L, lo in levels():
                    if L < C:
                        x = xl_rows[h % 2][k][:, tok]
                        nc.tensor.matmul(ps[0:C, 4 + 2 * (c % 2) + k // 4, P * (k % 4):P * (k % 4) + C], x, x,
                                         start=True, stop=True)
                nc.tensor.matmul(ps[0:C, 5 + 2 * (c % 2), 3 * P:3 * P + C], qq[:, 4 + h, tok], qq[:, h, tok],
                                 start=True, stop=True).then_inc(gp_ready, 1)

            for h in range(GH):
                level_products(h, 0)
                for c in range(5):
                    tok, C = chunk(c)
                    u = 5 * h + c
                    if c < 4:
                        level_products(h, c + 1)
                        if c:
                            pe.wait_ge(gt_copied, 4 * h + c)
                        elif h:
                            pe.wait_ge(go_copied, h)
                        nc.tensor.transpose(ps[0:C, 2, P:2 * P], khs[h][:, tok], ident).then_inc(gt_ready, 1)
                    pe.wait_ge(ga_ready, u + 1)
                    if c:
                        pe.wait_ge(gs_done, 4 * h + c)
                    else:
                        pe.wait_ge(gt_copied, 4 * h + 1)
                    for v in range(2):
                        f = GDV * h + P * v
                        o = ps[:, 2, NM * v:NM * v + NM] if c == 0 else ps[:, v, P * (c - 1):P * c]
                        ins = nc.tensor.matmul(o, vt[0:C, c, f:f + P], amat[c % 2][0:C, 0:C], start=True,
                                               stop=(c == 0))
                        if c:
                            ins = nc.tensor.matmul(o, state[(c - 1) % 2][:, P * v:P * v + P], qcs[h][:, tok],
                                                   start=False, stop=True)
                    if c < 4:
                        pe.wait_ge(gt_copied, 4 * h + c + 1)
                        nc.tensor.matmul(ps[:, 3, 0:GDV], ktok[c % 2][0:C, :], vt[0:C, c, GDV * h:GDV * h + GDV],
                                         start=True, stop=True).then_inc(gs_ready, 1)
                    else:
                        ins.then_inc(go_ready, 1)
            for h in range(GH):
                if h >= 2:
                    pe.wait_ge(root_ready, N_ROOTS + h - 1)
                sum_rows(4 + 2 * (h % 2), 2, T)
            strips(START["gla_gate"], KC, "x", T)
            strip(pos(START["gla_out"], 0), "x", T)
            strip(pos(START["gla_out"], 1), "b", T, ready=(b_ready, 7 * KC + SH))
            with pe.Fori(1, KC) as i:
                strip(pos(START["gla_out"], 0, i), "x", T)
                strip(pos(START["gla_out"], 1, i), "b", T)
            strips_and_sums(START["w_o"], "x", T, (x_ready, 4 * KC))
            pe.wait_ge(root_ready, N_ROOTS + GH + 1)
            sum_rows(4, KC, T)
            done = 8 * KC + SH
            for g, n_g in enumerate(FFN2_GROUPS):
                B = START[f"glu{g}up"]
                for k in range(4):
                    strip(pos(B, k), "x", SEQ if k % 2 else T, ready=(x_ready, 5 * KC) if g == k == 0 else None)
                with pe.Fori(1, n_g // 2) as i:
                    for k in range(4):
                        strip(pos(B, k, i, 4), "x", SEQ if k % 2 else T)
                B = START[f"glu{g}down"]
                if g == len(FFN2_GROUPS) - 1:
                    strips_and_sums(B, "b", SEQ, (b_ready, done), chunks=range(n_g))
                    break
                strip(pos(B, 0), "b", SEQ, chunks=range(n_g), ready=(b_ready, done))
                strip(pos(B, 1), "b", SEQ, chunks=range(n_g))
                with pe.Fori(1, KC // 2) as i:
                    for j in range(2):
                        strip(pos(B, j, i), "b", SEQ, chunks=range(n_g))
                done += n_g

        @block.gpsimd
        def _(pool):
            for h in range(RH + DH):
                if h == 0:
                    pool.wait_ge(b_ready, KC)
                elif h == RH:
                    pool.wait_ge(b_ready, 2 * KC)
                elif 1 < h < RH:
                    pool.wait_ge(rs_masked, 5 * (h - 1))
                elif h > RH + 1:
                    pool.wait_ge(ds_ready, 8 * (h - RH - 1))
                pool.dma_start(tbl[h % 2], tables[h]).then_inc(table_in[h % 2], 16)
            nc.gpsimd.memset(negm[:], 0.0).then_inc(pool_self, 1)
            pool.wait_ge(pool_self, 1)
            nc.gpsimd.affine_select(out=negm[:], in_=negm[:], compare_op=ALU.is_gt, fill=-1e30, base=0,
                                    pattern=[[1, P]], channel_multiplier=-1).then_inc(pool_self, 1)
            pool.wait_ge(params_in, 48)
            pool.wait_ge(pool_self, 2)
            nc.gpsimd.tensor_copy(identb[:], ident).then_inc(masks_made, 1)

            for h in range(GH):
                pool.wait_ge(gcum_done, 2 * h + 1)
                for k, L, lo in levels():
                    m = 7 * h + k
                    if m >= 2:
                        pool.wait_ge(gx_ready, m - 1)
                    d, s_ = halves(grow[m % 2], L, lo), halves(cums[h % 2], L, lo)
                    n = (T - lo) // (2 * L)
                    mid = s_[:, :, 0, L - 1:L].to_broadcast([P, n, L])
                    nc.gpsimd.tensor_tensor(d[:, :, 0, :], mid, s_[:, :, 0, :], ALU.subtract)
                    nc.gpsimd.tensor_tensor(d[:, :, 1, :], s_[:, :, 1, :], mid, ALU.subtract).then_inc(gd_ready, 1)



def feature_tiles(a):
    return np.ascontiguousarray(a.reshape(-1, P, a.shape[-1]).transpose(1, 0, 2))


def strips_of(w, cols):
    return [w[:, c:c + P].reshape(-1, P, P).transpose(1, 0, 2) for c in cols]


def weight_strips(a):
    w = a["w_in"][0]
    rq, rk, rv, rg, dq, dk, dv, cb, cc, cx, gates = (0, 512, 1024, 2048, 3072, 4096, 5120, 6144, 7168, 8192, 9216)
    s = []

    def tiles(w, first, n):
        return strips_of(w, range(first, first + P * n, P))

    def woven(*lists):
        return [x for group in zip(*lists) for x in group]

    s += woven(tiles(w, cc, 8), tiles(w, cx, 8), tiles(w, cb, 8))
    s += woven(tiles(w, gates + 2 * D, 8), tiles(a["w_branch"][0, 2], 0, 8))
    s += tiles(w, rq, 4) + tiles(w, rk, 4) + tiles(w, rv, 8) + tiles(w, rg, 8)
    s += woven(tiles(w, gates, 8), tiles(a["w_branch"][0, 0], 0, 8))
    s += tiles(w, dq, 8) + tiles(w, dk, 8) + tiles(w, dv, 8)
    s += woven(tiles(w, gates + D, 8), tiles(a["w_branch"][0, 1], 0, 8))
    s += tiles(a["w_out"][0], 0, 8)
    for g in range(4):
        s += tiles(a["w_up"][0], g * D, 8) + tiles(a["w_down"][0][g * D:g * D + D], 0, 8)
    s += second_strips(a, tiles, woven)
    s.append(np.zeros((P, KC, P), np.float32))
    out = np.empty((len(s), P, KC, P), np.float32)
    for i, x in enumerate(s):
        out[i, :, :x.shape[1]] = x
        out[i, :, x.shape[1]:] = 0
    return out


def second_strips(a, tiles, woven):
    w = a["w_in_2"][0]
    sq, sk, sv, gq, gk, gv, gr, lr, mg = (0, 512, 1024, 1536, 2048, 2560, 3584, 4608, 4624)
    s = tiles(w, sq, 4) + tiles(w, sk, 4) + tiles(w, sv, 4)
    s += woven(tiles(w, mg, 8), tiles(a["w_sb_out_2"][0], 0, 8))
    low = np.zeros((D, P), np.float32)
    low[:, :NM] = w[:, lr:lr + NM]
    s += tiles(low, 0, 1) + tiles(w, gq, 4) + tiles(w, gk, 4) + tiles(w, gv, 8)
    s += tiles(w, gr + 4 * P, 4) + tiles(w, gr, 4)
    s += woven(tiles(w, mg + D, 8), [np.roll(x, 4, axis=1) for x in tiles(a["w_gla_out_2"][0], 0, 8)])
    s += tiles(a["w_o_2"][0], 0, 8)
    first = 0
    for n in FFN2_GROUPS:
        s += woven(tiles(a["w_ffn_up_2"][0], first, n), tiles(a["w_ffn_gate_2"][0], first, n))
        s += tiles(a["w_ffn_down_2"][0][first:first + P * n], 0, 8)
        first += P * n
    return s


def gla_level_masks():
    s, t = np.arange(P)[:, None], np.arange(P)[None, :]
    m = [(s // (2 * L) == t // (2 * L)) & (s & L == 0) & (t & L != 0) for L in (64, 32, 16, 8, 4, 2, 1)]
    return np.ascontiguousarray(np.stack(m + [s == t]).astype(np.float32).transpose(1, 0, 2))


def shape_tables():
    j, p = np.arange(T)[None, :], np.arange(P)[:, None]
    log_g = np.log1p(-np.exp2(-5.0 - np.arange(RH)))
    decay = [np.where(j >= p, np.exp(g * np.maximum(j - p, 0)), 0.0) for g in log_g]
    dist = p + 3 * P + NM - j
    slopes = np.exp2(-8.0 / DH * (np.arange(DH) + 1.0))
    alibi = [np.where(dist >= 0, -s * DHD ** 0.5 * dist, -1e30) for s in slopes]
    return np.stack(decay + alibi).astype(np.float32)


def shape_consts():
    i, j = np.arange(P)[:, None], np.arange(P)[None, :]
    return np.ascontiguousarray(np.stack([i == j, i >= 0 * j, -(i >= j).astype(int), -(i >= 0 * j).astype(int)]).astype(
        np.float32).transpose(1, 0, 2))


def columns(a):
    c = []
    for name, (_, n) in COLS.items():
        v = a[name]
        if name == "conv_w":
            c.append(v[0].reshape(3, KC, P).transpose(2, 1, 0).reshape(P, -1))
        elif name == "conv_w_2":
            c.append(v[0].reshape(3, FT2, P).transpose(2, 1, 0).reshape(P, -1))
        else:
            c.append(v.reshape(n, P).T)
    return np.ascontiguousarray(np.concatenate(c, axis=1))


def device_inputs(a):
    return {
        "weights": weight_strips(a),
        "cols": columns(a),
        "tables": shape_tables(),
        "consts": shape_consts(),
        "lam_rows": np.ascontiguousarray(np.broadcast_to(a["diff_lambda"].reshape(1, -1), (P, 4 * DHD))),
        "x_t": feature_tiles(np.concatenate([a["meta_tokens"], a["x"][0]], axis=0).T),
        "meta2_t": feature_tiles(np.ascontiguousarray(a["meta_tokens_2"].T)),
        "gla_masks": gla_level_masks(),
        "wgk": np.ascontiguousarray(a["w_gk_up_2"][0]),
    }


def kernel(**inputs):
    import concourse.bacc as bacc
    from concourse.bass_utils import run_bass_kernel_spmd

    arrays = device_inputs({k: np.asarray(v) for k, v in inputs.items()})
    nc = bacc.Bacc("TRN2", target_bir_lowering=False, num_devices=1)
    args = {n: nc.dram_tensor(f"{n}_dram", v.shape, F32, kind="ExternalInput").ap() for n, v in arrays.items()}
    res_dram = nc.dram_tensor("res_dram", [P, KC, T], F32).ap()
    mrg_dram = nc.dram_tensor("mrg_dram", [P, KC, T], F32).ap()
    out = nc.dram_tensor("out_dram", [P, KC, SEQ], F32, kind="ExternalOutput").ap()
    build(nc, res_dram=res_dram, mrg_dram=mrg_dram, out=out, **args)
    r = run_bass_kernel_spmd(nc, [{f"{n}_dram": v for n, v in arrays.items()}], core_ids=[0])
    got = r.results[0]["out_dram"]
    return np.ascontiguousarray(got.transpose(2, 1, 0).reshape(1, SEQ, D))
```
